# Optimizing a Trainium2 kernel written in Bass

```python
import math
import jax, jax.numpy as jnp
from jax import lax
import numpy as np

"""Two post-norm (DeepNorm) layers of a hybrid diffusion / flow-matching backbone.

Each layer has two sub-layers:
  1. a parallel head-group token mixer. One combined input projection feeds two head groups:
     4 differential-attention heads (512 wide) and 8-query / 2-kv grouped-query attention
     heads with q/k RMS-norm (512 wide). Both use 2-D axial rotary on latent tokens. The two
     group outputs are concatenated and passed through one output projection.
  2. a channel mixer: dense SwiGLU on even layers, top-2-of-8 expert SwiGLU on odd layers.
AdaLN shift/scale/gate comes from SiLU(c) for latent tokens and from SiLU(c_ctx) for context
tokens. Residual update: x <- LayerNorm(alpha*x + gate*sublayer(x*(1+scale)+shift)).
Context tokens attend only to context tokens and carry no position. Latent tokens attend in one
softmax to all latent keys plus all cached context keys.

Inputs:
  x_prompt  (BATCH, SEQ, D_MODEL)            context tokens of new requests (group i)
  x_sample  (DEC_BATCH, DEC_SEQ, D_MODEL)    noisy latent grid tokens (group ii)
  cache_a_k (DEC_BATCH, DEPTH, PAST_LEN, DIFF_HEADS, 2, HEAD_DIM)  diff-attn context keys (k1,k2)
  cache_a_v (DEC_BATCH, DEPTH, PAST_LEN, DIFF_HEADS, 2*HEAD_DIM)   diff-attn context values
  cache_b_k (DEC_BATCH, DEPTH, PAST_LEN, GQA_KV_HEADS, HEAD_DIM)   GQA context keys (RMS-normed)
  cache_b_v (DEC_BATCH, DEPTH, PAST_LEN, GQA_KV_HEADS, HEAD_DIM)   GQA context values
  c (DEC_BATCH, D_MODEL) conditioning; c_ctx (D_MODEL,) learned context modulation vector; weights.
Output tuple:
  (y_prompt (BATCH, SEQ, D_MODEL),
   y_sample (DEC_BATCH, DEC_SEQ, D_MODEL),
   new_cache_a_k (BATCH, DEPTH, SEQ, DIFF_HEADS, 2, HEAD_DIM),
   new_cache_a_v (BATCH, DEPTH, SEQ, DIFF_HEADS, 2*HEAD_DIM),
   new_cache_b_k (BATCH, DEPTH, SEQ, GQA_KV_HEADS, HEAD_DIM),
   new_cache_b_v (BATCH, DEPTH, SEQ, GQA_KV_HEADS, HEAD_DIM))
"""

D_MODEL = 1024
BATCH = 1
SEQ = 128
DEPTH = 2
DEC_BATCH = 1
DEC_SEQ = 256
PAST_LEN = 128

GRID_W = 64
HEAD_DIM = 64
DIFF_HEADS = 4
GQA_HEADS = 8
GQA_KV_HEADS = 2
GQA_GROUP = GQA_HEADS // GQA_KV_HEADS
DIFF_WIDTH = DIFF_HEADS * 2 * HEAD_DIM
GQA_WIDTH = GQA_HEADS * HEAD_DIM
KV_WIDTH = GQA_KV_HEADS * HEAD_DIM
MIX_WIDTH = DIFF_WIDTH + GQA_WIDTH
IN_COLS = 3 * DIFF_WIDTH + GQA_WIDTH + 2 * KV_WIDTH
IN_SPLITS = (DIFF_WIDTH, 2 * DIFF_WIDTH, 3 * DIFF_WIDTH,
             3 * DIFF_WIDTH + GQA_WIDTH, 3 * DIFF_WIDTH + GQA_WIDTH + KV_WIDTH)
D_FF = 2816
N_EXPERTS = 8
TOP_K = 2
N_DENSE = (DEPTH + 1) // 2
N_MOE = DEPTH // 2
Q_BLOCK = 128
ROPE_THETA = 10000.0
EPS = 1e-6
DEEPNORM_ALPHA = (2 * DEPTH) ** 0.25
DEEPNORM_BETA = (8 * DEPTH) ** -0.25

kernel_name = "hybrid_diffusion_diffattn_gqa_moe_step"

def layer_norm(x, g, b):
    xf = x.astype(jnp.float32)
    mu = jnp.mean(xf, axis=-1, keepdims=True)
    var = jnp.mean(jnp.square(xf - mu), axis=-1, keepdims=True)
    return ((xf - mu) * lax.rsqrt(var + EPS)).astype(x.dtype) * g + b

def rms_norm(x, g):
    xf = x.astype(jnp.float32)
    return (xf * lax.rsqrt(jnp.mean(xf * xf, axis=-1, keepdims=True) + EPS)).astype(x.dtype) * g

def axial_rope_tables(n_tokens, dtype):
    rows = n_tokens // GRID_W
    row = jnp.repeat(jnp.arange(rows, dtype=jnp.float32), GRID_W)
    col = jnp.tile(jnp.arange(GRID_W, dtype=jnp.float32), rows)
    n_freq = HEAD_DIM // 4
    inv = ROPE_THETA ** (-jnp.arange(n_freq, dtype=jnp.float32) / n_freq)
    ar = row[:, None] * inv
    ac = col[:, None] * inv
    ang = jnp.concatenate([ar, ar, ac, ac], axis=-1)
    return jnp.cos(ang).astype(dtype), jnp.sin(ang).astype(dtype)

def apply_axial_rope(x, cos, sin):
    x1, x2, x3, x4 = jnp.split(x, 4, axis=-1)
    rot = jnp.concatenate([-x2, x1, -x4, x3], axis=-1)
    shape = (1, cos.shape[0]) + (1,) * (x.ndim - 3) + (HEAD_DIM,)
    return x * cos.reshape(shape) + rot * sin.reshape(shape)

def sweep_query_blocks(fn, q):
    b, n = q.shape[:2]
    nb = n // Q_BLOCK
    blocks = jnp.moveaxis(q.reshape((b, nb, Q_BLOCK) + q.shape[2:]), 1, 0)
    out = lax.map(fn, blocks)
    return jnp.moveaxis(out, 0, 1).reshape((b, n) + out.shape[3:])

def diff_lambda_value(lp, lam_init):
    lpf = lp.astype(jnp.float32)
    return jnp.exp(jnp.sum(lpf[0] * lpf[1])) - jnp.exp(jnp.sum(lpf[2] * lpf[3])) + lam_init

def diff_attention(q, k, v, lam):
    scale = HEAD_DIM ** -0.5
    def block(qb):
        s = jnp.einsum('bqhcd,bkhcd->bchqk', qb, k).astype(jnp.float32) * scale
        p = jax.nn.softmax(s, axis=-1)
        a = p[:, 0] - lam * p[:, 1]
        return jnp.einsum('bhqk,bkhe->bqhe', a.astype(v.dtype), v)
    return sweep_query_blocks(block, q)

def gqa_attention(q, k, v):
    scale = HEAD_DIM ** -0.5
    def block(qb):
        b, nq = qb.shape[:2]
        qg = qb.reshape(b, nq, GQA_KV_HEADS, GQA_GROUP, HEAD_DIM)
        s = jnp.einsum('bqkgd,btkd->bkgqt', qg, k).astype(jnp.float32) * scale
        p = jax.nn.softmax(s, axis=-1).astype(v.dtype)
        o = jnp.einsum('bkgqt,btkd->bqkgd', p, v)
        return o.reshape(b, nq, GQA_HEADS, HEAD_DIM)
    return sweep_query_blocks(block, q)

def project_heads(h, w_in, qk_gain):
    b, n, _ = h.shape
    a_q, a_k, a_v, b_q, b_k, b_v = jnp.split(h @ w_in, list(IN_SPLITS), axis=-1)
    a_q = a_q.reshape(b, n, DIFF_HEADS, 2, HEAD_DIM)
    a_k = a_k.reshape(b, n, DIFF_HEADS, 2, HEAD_DIM)
    a_v = a_v.reshape(b, n, DIFF_HEADS, 2 * HEAD_DIM)
    b_q = rms_norm(b_q.reshape(b, n, GQA_HEADS, HEAD_DIM), qk_gain[0])
    b_k = rms_norm(b_k.reshape(b, n, GQA_KV_HEADS, HEAD_DIM), qk_gain[1])
    b_v = b_v.reshape(b, n, GQA_KV_HEADS, HEAD_DIM)
    return a_q, a_k, a_v, b_q, b_k, b_v

def mixer_output(a_q, a_k, a_v, b_q, b_k, b_v, lam, lam_init, subln_gain, w_out):
    o_a = rms_norm(diff_attention(a_q, a_k, a_v, lam), subln_gain) * (1.0 - lam_init)
    o_b = gqa_attention(b_q, b_k, b_v)
    b, n = o_a.shape[:2]
    o = jnp.concatenate([o_a.reshape(b, n, DIFF_WIDTH), o_b.reshape(b, n, GQA_WIDTH)], axis=-1)
    return o @ w_out

def ada_modulation(cond, w_ada, b_ada):
    m = jax.nn.silu(cond) @ w_ada + b_ada
    return jnp.split(m[..., None, :], 6, axis=-1)

def swiglu(h, wg, wu, wd):
    return (jax.nn.silu(h @ wg) * (h @ wu)) @ wd

def moe_swiglu(h, w_router, wg, wu, wd):
    logits = (h @ w_router).astype(jnp.float32)
    top_v, top_i = lax.top_k(logits, TOP_K)
    top_p = jax.nn.softmax(top_v, axis=-1)
    gates = jnp.sum(jax.nn.one_hot(top_i, N_EXPERTS, dtype=jnp.float32) * top_p[..., None], axis=-2)
    act = jax.nn.silu(jnp.einsum('bnd,edf->bnef', h, wg)) * jnp.einsum('bnd,edf->bnef', h, wu)
    act = act * gates.astype(h.dtype)[..., None]
    return jnp.einsum('bnef,efd->bnd', act, wd)

def channel_mixer(l, h, w_ffn_gate, w_ffn_up, w_ffn_down, w_router, w_moe_gate, w_moe_up, w_moe_down):
    if l % 2 == 0:
        i = l // 2
        return swiglu(h, w_ffn_gate[i], w_ffn_up[i], w_ffn_down[i])
    i = l // 2
    return moe_swiglu(h, w_router[i], w_moe_gate[i], w_moe_up[i], w_moe_down[i])

def setup_inputs(seed: int = 0) -> dict:
    key = jax.random.key(seed)
    ks = jax.random.split(key, 24)
    nrm = jax.random.normal
    f32 = jnp.float32
    col_scale = jnp.concatenate([
        jnp.ones((2 * DIFF_WIDTH,), f32), jnp.full((DIFF_WIDTH,), DEEPNORM_BETA, f32),
        jnp.ones((GQA_WIDTH + KV_WIDTH,), f32), jnp.full((KV_WIDTH,), DEEPNORM_BETA, f32)])
    return {
        "x_prompt": nrm(ks[0], (BATCH, SEQ, D_MODEL), f32),
        "x_sample": nrm(ks[1], (DEC_BATCH, DEC_SEQ, D_MODEL), f32),
        "cache_a_k": nrm(ks[2], (DEC_BATCH, DEPTH, PAST_LEN, DIFF_HEADS, 2, HEAD_DIM), f32),
        "cache_a_v": 0.5 * nrm(ks[3], (DEC_BATCH, DEPTH, PAST_LEN, DIFF_HEADS, 2 * HEAD_DIM), f32),
        "cache_b_k": nrm(ks[4], (DEC_BATCH, DEPTH, PAST_LEN, GQA_KV_HEADS, HEAD_DIM), f32),
        "cache_b_v": 0.5 * nrm(ks[5], (DEC_BATCH, DEPTH, PAST_LEN, GQA_KV_HEADS, HEAD_DIM), f32),
        "c": nrm(ks[6], (DEC_BATCH, D_MODEL), f32),
        "c_ctx": nrm(ks[7], (D_MODEL,), f32),
        "w_ada": nrm(ks[8], (DEPTH, D_MODEL, 6 * D_MODEL), f32) * D_MODEL ** -0.5,
        "b_ada": 0.01 * nrm(ks[9], (DEPTH, 6 * D_MODEL), f32),
        "w_in": nrm(ks[10], (DEPTH, D_MODEL, IN_COLS), f32) * D_MODEL ** -0.5 * col_scale,
        "w_out": nrm(ks[11], (DEPTH, MIX_WIDTH, D_MODEL), f32) * MIX_WIDTH ** -0.5 * DEEPNORM_BETA,
        "diff_lambda": 0.1 * nrm(ks[12], (DEPTH, 4, HEAD_DIM), f32),
        "diff_subln": 1.0 + 0.02 * nrm(ks[13], (DEPTH, 2 * HEAD_DIM), f32),
        "qk_norm_gain": 1.0 + 0.02 * nrm(ks[14], (DEPTH, 2, HEAD_DIM), f32),
        "ln_gain": 1.0 + 0.02 * nrm(ks[15], (DEPTH, 2, D_MODEL), f32),
        "ln_bias": 0.02 * nrm(ks[16], (DEPTH, 2, D_MODEL), f32),
        "w_ffn_gate": nrm(ks[17], (N_DENSE, D_MODEL, D_FF), f32) * D_MODEL ** -0.5,
        "w_ffn_up": nrm(ks[18], (N_DENSE, D_MODEL, D_FF), f32) * D_MODEL ** -0.5,
        "w_ffn_down": nrm(ks[19], (N_DENSE, D_FF, D_MODEL), f32) * D_FF ** -0.5 * DEEPNORM_BETA,
        "w_router": nrm(ks[20], (N_MOE, D_MODEL, N_EXPERTS), f32) * D_MODEL ** -0.5,
        "w_moe_gate": nrm(ks[21], (N_MOE, N_EXPERTS, D_MODEL, D_FF), f32) * D_MODEL ** -0.5,
        "w_moe_up": nrm(ks[22], (N_MOE, N_EXPERTS, D_MODEL, D_FF), f32) * D_MODEL ** -0.5,
        "w_moe_down": nrm(ks[23], (N_MOE, N_EXPERTS, D_FF, D_MODEL), f32) * D_FF ** -0.5 * DEEPNORM_BETA,
    }

def reference(x_prompt, x_sample, cache_a_k, cache_a_v, cache_b_k, cache_b_v, c, c_ctx,
              w_ada, b_ada, w_in, w_out, diff_lambda, diff_subln, qk_norm_gain, ln_gain, ln_bias,
              w_ffn_gate, w_ffn_up, w_ffn_down, w_router, w_moe_gate, w_moe_up, w_moe_down):
    rope_cos, rope_sin = axial_rope_tables(x_sample.shape[1], x_sample.dtype)
    xp, xs = x_prompt, x_sample
    ctx_a_k, ctx_a_v, ctx_b_k, ctx_b_v = [], [], [], []
    for l in range(DEPTH):
        lam_init = 0.8 - 0.6 * math.exp(-0.3 * l)
        lam = diff_lambda_value(diff_lambda[l], lam_init)
        p_sh1, p_sc1, p_g1, p_sh2, p_sc2, p_g2 = ada_modulation(c_ctx, w_ada[l], b_ada[l])
        s_sh1, s_sc1, s_g1, s_sh2, s_sc2, s_g2 = ada_modulation(c, w_ada[l], b_ada[l])

        hp = xp * (1 + p_sc1) + p_sh1
        a_q, a_k, a_v, b_q, b_k, b_v = project_heads(hp, w_in[l], qk_norm_gain[l])
        ctx_a_k.append(a_k)
        ctx_a_v.append(a_v)
        ctx_b_k.append(b_k)
        ctx_b_v.append(b_v)
        mix_p = mixer_output(a_q, a_k, a_v, b_q, b_k, b_v, lam, lam_init, diff_subln[l], w_out[l])
        xp = layer_norm(DEEPNORM_ALPHA * xp + p_g1 * mix_p, ln_gain[l, 0], ln_bias[l, 0])

        hs = xs * (1 + s_sc1) + s_sh1
        a_q, a_k, a_v, b_q, b_k, b_v = project_heads(hs, w_in[l], qk_norm_gain[l])
        a_q = apply_axial_rope(a_q, rope_cos, rope_sin)
        a_k = apply_axial_rope(a_k, rope_cos, rope_sin)
        b_q = apply_axial_rope(b_q, rope_cos, rope_sin)
        b_k = apply_axial_rope(b_k, rope_cos, rope_sin)
        a_k = jnp.concatenate([a_k, cache_a_k[:, l]], axis=1)
        a_v = jnp.concatenate([a_v, cache_a_v[:, l]], axis=1)
        b_k = jnp.concatenate([b_k, cache_b_k[:, l]], axis=1)
        b_v = jnp.concatenate([b_v, cache_b_v[:, l]], axis=1)
        mix_s = mixer_output(a_q, a_k, a_v, b_q, b_k, b_v, lam, lam_init, diff_subln[l], w_out[l])
        xs = layer_norm(DEEPNORM_ALPHA * xs + s_g1 * mix_s, ln_gain[l, 0], ln_bias[l, 0])

        hp = xp * (1 + p_sc2) + p_sh2
        ffn_p = channel_mixer(l, hp, w_ffn_gate, w_ffn_up, w_ffn_down,
                              w_router, w_moe_gate, w_moe_up, w_moe_down)
        xp = layer_norm(DEEPNORM_ALPHA * xp + p_g2 * ffn_p, ln_gain[l, 1], ln_bias[l, 1])
        hs = xs * (1 + s_sc2) + s_sh2
        ffn_s = channel_mixer(l, hs, w_ffn_gate, w_ffn_up, w_ffn_down,
                              w_router, w_moe_gate, w_moe_up, w_moe_down)
        xs = layer_norm(DEEPNORM_ALPHA * xs + s_g2 * ffn_s, ln_gain[l, 1], ln_bias[l, 1])

    new_cache_a_k = jnp.stack(ctx_a_k, axis=1)
    new_cache_a_v = jnp.stack(ctx_a_v, axis=1)
    new_cache_b_k = jnp.stack(ctx_b_k, axis=1)
    new_cache_b_v = jnp.stack(ctx_b_v, axis=1)
    return (xp, xs, new_cache_a_k, new_cache_a_v, new_cache_b_k, new_cache_b_v)


_drawn_inputs = setup_inputs


def setup_inputs(seed=0):
    import zlib

    import numpy as np

    out = dict(_drawn_inputs(seed))
    spreads = {}
    factors = {'cache_b_k': 6.212,
     'cache_b_v': 5.688,
     'b_ada': 3.907,
     'diff_lambda': 4.193,
     'diff_subln': 6.704,
     'qk_norm_gain': 2.697}
    for name, (base, spread) in spreads.items():
        noise = np.random.default_rng([zlib.crc32(name.encode()), seed]).standard_normal(out[name].shape)
        drawn = base * np.exp(spread * noise) if base else spread * noise
        out[name] = __import__('jax').numpy.asarray(drawn.astype(out[name].dtype))
    for name, factor in factors.items():
        out[name] = (out[name] * factor).astype(out[name].dtype)
    return out
```

```python
import math
from contextlib import ExitStack

import numpy as np
import concourse.bass as bass
from concourse import mybir

F32 = mybir.dt.float32
I32 = mybir.dt.int32
ALU = mybir.AluOpType
ACT = mybir.ActivationFunctionType
AX = mybir.AxisListType.X

P = 128
D = 1024
KD = D // P
DEPTH = 2
NT = 3
HD = 64
DH, GH, GKV = 4, 8, 2
DW = DH * 2 * HD
GW = GH * HD
KVW = GKV * HD
COLS = 3 * DW + GW + 2 * KVW
AQ, AK, AV, BQ, BK, BV = 0, DW, 2 * DW, 3 * DW, 3 * DW + GW, 3 * DW + GW + KVW
F = 2816
FC = 256
NCH = F // FC
NE = 8
GRID_W = 64
EPS = 1e-6
ALPHA = (2 * DEPTH) ** 0.25
SCALE = HD ** -0.5
TOKENS = NT * P
BT = 64
MAX_BLOCKS = TOKENS // BT
MAX_PAIRS = MAX_BLOCKS // 2
GU_SLOTS = 3
D_SLOTS = 3
GU_USES = [4, 4, 3]
UNITS = 24
NGROUPS = 14
POSTS = [(0, 1), (0, 2), (1, 1), (1, 2), (3, 0), (3, 1), (3, 2), (4, 0), (4, 1), (4, 2)]
GROUPS = [(0, 0), (0, 1), (0, 2), (1, 0), (1, 1), (1, 2), ("ca", 0), ("cb", 0),
          (3, 0), (3, 1), (3, 2), (4, 0), (4, 1), (4, 2)]
PIECE_COLS = [(0, 512), (512, 512), (1024, 512), (1536, 512), (2048, 256)]

C_ID, C_UP, C_ONES = 0, 128, 256
C_COS, C_SIN = 384, 512
C_SEL = 640
C_PIECE = 896
C_LOW = 920
C_IOTA = 984
C_END = C_IOTA + TOKENS


def shape_constants():
    c = np.zeros((P, C_END), np.float32)
    r = np.arange(P)
    c[:, C_ID:C_ID + P] = np.eye(P)
    c[:, C_UP:C_UP + P] = r[:, None] < r[None, :]
    c[:, C_IOTA:C_IOTA + TOKENS] = np.arange(TOKENS)
    c[:, C_ONES:C_ONES + P] = 1
    n_freq = HD // 4
    inv = np.float32(10000.0) ** (-np.arange(n_freq, dtype=np.float32) / n_freq)
    pos = np.arange(2 * P)
    ar = (pos // GRID_W).astype(np.float32)[:, None] * inv
    ac = (pos % GRID_W).astype(np.float32)[:, None] * inv
    ang = np.concatenate([ar, ar, ac, ac], axis=-1)
    sign = np.repeat(np.array([-1, 1, -1, 1], np.float32), n_freq)
    c[:, C_COS:C_COS + 2 * HD] = np.cos(ang).reshape(2, P, HD).transpose(1, 0, 2).reshape(P, -1)
    c[:, C_SIN:C_SIN + 2 * HD] = (np.sin(ang) * sign).reshape(2, P, HD).transpose(1, 0, 2).reshape(P, -1)
    for k in range(2):
        c[k, C_SEL + k * P:C_SEL + (k + 1) * P] = 1
    for j in range(12):
        c[j, C_PIECE + 2 * j:C_PIECE + 2 * j + 2] = 1
    e = np.arange(NE)
    c[:, C_LOW:C_LOW + 64] = (e[None, :] < e[:, None]).reshape(-1)
    return c


def tile_of_unit(v):
    return v // 8, v % 8


def gqa_before(u):
    return u // 8 * 4 + max(0, u % 8 - 4)


def ada_expands_before(j):
    return [0, 1, 2, 3, 4, 6, 8, 9, 10, 11, 12, 12][j]


def build(nc, x_prompt, x_sample, cache_a_k, cache_a_v, cache_b_k, cache_b_v, c, c_ctx, w_ada,
          b_ada, w_in, w_out, diff_lambda, diff_subln, qk_norm_gain, ln_gain, ln_bias, w_ffn_gate,
          w_ffn_up, w_ffn_down, w_router, w_moe_gate, w_moe_up, w_moe_down, consts,
          y_prompt, y_sample, new_a_k, new_a_v, new_b_k, new_b_v):
    ctx = ExitStack()
    with ctx:
        def sb(name, shape, dt=F32):
            return ctx.enter_context(nc.sbuf_tensor(name, shape, dt))

        def sem(name):
            return ctx.enter_context(nc.semaphore(name))

        gu_ring = sb("gu_ring", [P, GU_SLOTS, KD * 512])
        d_ring = sb("d_ring", [P, D_SLOTS, 2 * D])
        cst = sb("cst", [P, C_END])
        x = sb("x", [P, NT, D])
        hT = sb("hT", [P, KD, TOKENS])
        qkv = sb("qkv", [P, NT, COLS])
        scratch = sb("scratch", [P, 8704])
        cache_a = sb("cache_a", [P, 2, DW])
        cache_b = sb("cache_b", [P, 2, KVW])
        o = sb("o", [P, NT, D])
        gate = sb("gate", [P, 2, D])
        ada_row = sb("ada_row", [2, 512])
        gate2_rows = sb("gate2_rows", [2, 2, 512])
        mod = sb("mod", [P, 4, KD, 2])
        cond_raw = sb("cond_raw", [P, 2, KD])
        cond = sb("cond", [P, KD, 2])
        bada = sb("bada", [12, 512])
        lam_in = sb("lam_in", [P, 4, HD])
        lam_tmp = sb("lam_tmp", [P, 2, HD])
        lam_sum = sb("lam_sum", [P, 2])
        lam_exp = sb("lam_exp", [P, 2])
        neg_lam = sb("neg_lam", [P, 1])
        subln = sb("subln", [P, 2 * HD])
        qk_gain = sb("qk_gain", [P, 2, HD])
        smax = sb("smax", [P, 2, 2])
        nbias = sb("nbias", [P, 2, 2])
        rsum = sb("rsum", [P, 4, 2])
        rinv = sb("rinv", [P, 4, 2])
        rlam = sb("rlam", [P, 1])
        var_in = sb("var_in", [P, 8])
        rstd = sb("rstd", [P, 8])
        neg_half = sb("neg_half", [P, 8])
        stats = sb("stats", [P, 2, 6])
        mv = sb("mv", [P, 2])
        w_rt = sb("w_rt", [P, KD, NE])
        logit = sb("logit", [P, NT, NE])
        top = sb("top", [P, NT])
        expo = sb("expo", [P, NT, NE])
        pair = sb("pair", [P, NT * NE * NE])
        pair2 = sb("pair2", [P, NT * NE * NE])
        place = sb("place", [P, NT, NE])
        chosen = sb("chosen", [P, NT, NE])
        gates = sb("gates", [P, NT, NE])
        gsum = sb("gsum", [P, NT])
        rank = sb("rank", [P, NT, NE + 1])
        counts = sb("counts", [P, NE])
        blocks = sb("blocks", [P, NE + 1])
        cum = sb("cum", [P, NE + 1])
        pairs = sb("pairs", [P, NE])
        pair_cum = sb("pair_cum", [P, NE])
        sched = sb("sched", [P, 3 * NE + 2], I32)
        squares = sb("squares", [P, 768])
        pick_g = squares[:, :].rearrange("p (s i t) -> p s i t", s=2, i=NT)

        qT = scratch[:, 0:3072].rearrange("p (h t) -> p h t", h=8)
        kT = scratch[:, 3072:5632].rearrange("p (h t) -> p h t", h=5)
        prob = scratch[:, 5632:7168].rearrange("p (s c k) -> p s c k", s=2, c=2)
        pT = scratch[:, 7168:8704].rearrange("p (s c k) -> p s c k", s=2, c=2)
        y_sb = scratch[:, 0:3072].rearrange("p (b n f) -> p b n f", b=MAX_PAIRS, n=2)
        pick_gT = scratch[:, 3072:5376].rearrange("p (b n i t) -> p b n i t", b=MAX_PAIRS, n=2, i=NT)
        pick = scratch[:, 5376:6528].rearrange("p (i t) -> p i t", i=NT)
        sil = scratch[:, 6528:7040].rearrange("p (s f) -> p s f", s=2)
        hid = scratch[:, 7040:7552].rearrange("p (s f) -> p s f", s=2)
        hidT = scratch[:, 7552:8064].rearrange("p (s f t) -> p s f t", s=2, f=2)
        o_flat = o[:, :, :].rearrange("p i d -> p (i d)")
        ln_par = o_flat[:, 0:2 * D].rearrange("p (a d) -> p a d", a=2)
        mixed = o_flat[:, 2 * D:3 * D]
        xg_rows = o_flat[:, 2 * D:3 * D].rearrange("p (s n) -> p s n", s=2)
        rope_a = o_flat[:, 0:512]
        rope_b = o_flat[:, 512:1024]
        qkv_flat = qkv[:, :, :].rearrange("p i d -> p (i d)")
        y_acc = qkv_flat[:, 0:NT * D].rearrange("p (i d) -> p i d", i=NT)
        h_tok = qkv_flat[:, NT * D:2 * NT * D].rearrange("p (i d) -> p i d", i=NT)

        ps = ctx.enter_context(nc.psum_tensor("ps", [P, 8, 512], F32))
        ident = cst[:, C_ID:C_ID + P]

        first_loaded = sem("first_loaded")
        params_loaded = sem("params_loaded")
        ln_loaded = sem("ln_loaded")
        gu_landed = [sem(f"gu_landed{k}") for k in range(GU_SLOTS)]
        d_landed = [sem(f"d_landed{k}") for k in range(D_SLOTS)]
        stored = sem("stored")
        dve_step = sem("dve_step")
        silu_done = sem("silu_done")
        ada_mm = sem("ada_mm")
        ada_row_copied = sem("ada_row_copied")
        ada_expanded = sem("ada_expanded")
        ada_exp_copied = sem("ada_exp_copied")
        x_ready = sem("x_ready")
        xT_mm = sem("xT_mm")
        hT_act = sem("hT_act")
        hT_dve = sem("hT_dve")
        qkv_mm = sem("qkv_mm")
        qkv_copied = sem("qkv_copied")
        post_done = sem("post_done")
        var_ready = sem("var_ready")
        rstd_ready = sem("rstd_ready")
        lam_sums = sem("lam_sums")
        lam_exps = sem("lam_exps")
        qt_mm = sem("qt_mm")
        qt_copied = sem("qt_copied")
        s_mm = sem("s_mm")
        max_done = sem("max_done")
        exp_done = sem("exp_done")
        soft_done = sem("soft_done")
        pT_mm = sem("pT_mm")
        pT_act = sem("pT_act")
        pT_dve = sem("pT_dve")
        o_mm = sem("o_mm")
        o_copied = sem("o_copied")
        oT_mm = sem("oT_mm")
        oT_copied = sem("oT_copied")
        out_mm = sem("out_mm")
        gu_mm = sem("gu_mm")
        sil_ready = sem("sil_ready")
        hid_ready = sem("hid_ready")
        hidT_mm = sem("hidT_mm")
        hidT_copied = sem("hidT_copied")
        chunk_done = sem("chunk_done")
        router_loaded = sem("router_loaded")
        logit_mm = sem("logit_mm")
        top_ready = sem("top_ready")
        expo_ready = sem("expo_ready")
        chosen_ready = sem("chosen_ready")
        prefix_mm = sem("prefix_mm")
        sched_ready = sem("sched_ready")
        hTok_mm = sem("hTok_mm")
        hTok_copied = sem("hTok_copied")
        pick_ready = sem("pick_ready")
        pick_g_ready = sem("pick_g_ready")
        xg_rows_mm = sem("xg_rows_mm")
        xg_rows_copied = sem("xg_rows_copied")
        xgT_mm = sem("xgT_mm")
        xgT_copied = sem("xgT_copied")
        pgT_mm = sem("pgT_mm")
        pgT_copied = sem("pgT_copied")
        y_copied = sem("y_copied")
        spread_mm = sem("spread_mm")
        spread_added = sem("spread_added")

        gu_plan = []

        def ada_piece(l, j):
            src = w_ada[l].rearrange("(p k) n -> p k n", k=KD)[:, :, 512 * j:512 * j + 512]
            gu_plan.append((("w", src, 512), (ada_mm, 12 * l + j + 1)))

        DENSE = NT * NCH
        for l in range(DEPTH):
            for j in range(4):
                ada_piece(l, j)
            for n, (c0, w) in enumerate(PIECE_COLS):
                src = w_in[l].rearrange("(k p) n -> p k n", p=P)[:, :, c0:c0 + w]
                gu_plan.append((("w", src, w), (qkv_mm, 15 * l + 3 * n + 3)))
            for j in range(4, 12):
                ada_piece(l, j)
            for n in range(2):
                src = w_out[l].rearrange("(k p) n -> p k n", p=P)[:, :, 512 * n:512 * n + 512]
                gu_plan.append((("w", src, 512), (out_mm, 6 * l + 3 * n + 3)))
            if l == 0:
                for ch in range(NCH):
                    gu_plan.append((("f", ch, 0), (gu_mm, NT * ch + NT)))
        n_static = len(gu_plan)
        gu_slot = [(k - n_static + 2) % GU_SLOTS for k in range(n_static)]
        gu_value, used = [], [0] * GU_SLOTS
        for k in range(n_static):
            used[gu_slot[k]] += 1
            gu_value.append(32 * used[gu_slot[k]])
        gu_static = list(used)
        first_gu = {0: 0, 1: 19 + NCH}
        dense_gu = 19

        def piece_view(k, w=512):
            return gu_ring[:, gu_slot[k], 0:KD * w].rearrange("p (k n) -> p k n", k=KD)

        def chunk_view(slot):
            return gu_ring[:, slot, :].rearrange("p (k a f) -> p k a f", k=KD, a=2)

        def down_view(slot):
            return d_ring[:, slot, :].rearrange("p (f n) -> p f n", f=2)

        def gate_up_src(wg, wu, ch):
            return [w.rearrange("(k p) f -> p k f", p=P)[:, :, FC * ch:FC * ch + FC] for w in (wg, wu)]

        def down_src(wd, ch):
            return wd[FC * ch:FC * ch + FC, :].rearrange("(f p) n -> p f n", p=P)

        def each_block(eng, n_blocks, step):
            def rest(b):
                if b < MAX_BLOCKS:
                    with eng.If(n_blocks > b):
                        step(b)
                        rest(b + 1)
            step(0)
            rest(1)

        block = ctx.enter_context(nc.Block())

        @block.sync
        def _(sp):
            def load_chunk(slot, wg, wu, ch):
                for a, src in enumerate(gate_up_src(wg, wu, ch)):
                    sp.dma_start(chunk_view(slot)[:, :, a, :], src).then_inc(gu_landed[slot], 16)

            last_user = [None] * GU_SLOTS
            for k, ((kind, src, w), release) in enumerate(gu_plan):
                slot = gu_slot[k]
                if last_user[slot] is not None:
                    sp.wait_ge(*last_user[slot])
                last_user[slot] = release
                if kind == "w":
                    for a in range(2):
                        sp.dma_start(piece_view(k, w)[:, 4 * a:4 * a + 4, :],
                                     src[:, 4 * a:4 * a + 4, :]).then_inc(gu_landed[slot], 16)
                else:
                    load_chunk(slot, w_ffn_gate[0], w_ffn_up[0], src)
                    if src >= D_SLOTS:
                        sp.wait_ge(chunk_done, src - D_SLOTS + 1)
                    sp.dma_start(down_view(src % D_SLOTS), down_src(w_ffn_down[0], src)).then_inc(
                        d_landed[src % D_SLOTS], 16)
            sp.wait_ge(out_mm, 12)
            with sp.Fori(0, NE) as t:
                for ch in range(NCH):
                    before = ch - 3 if ch >= 3 else [9, 10, 8][ch] - NCH
                    sp.wait_ge(chunk_done, t * NCH + (NCH + before + 1))
                    load_chunk(ch % GU_SLOTS, w_moe_gate[0, t], w_moe_up[0, t], ch)
                    sp.dma_start(down_view(ch % D_SLOTS), down_src(w_moe_down[0, t], ch)).then_inc(
                        d_landed[ch % D_SLOTS], 16)

        @block.gpsimd
        def _(pool):
            n_rstd = [0]

            def rstds(n, width):
                for _ in range(n):
                    n_rstd[0] += 1
                    pool.wait_ge(var_ready, n_rstd[0])
                    pool.tensor_tensor(rstd[:, 0:width], var_in[:, 0:width], neg_half[:, 0:width],
                                       ALU.pow).then_inc(rstd_ready, 1)

            def load_params(l):
                src = [(lam_in[:, :, :], diff_lambda[l].rearrange("a d -> (a d)").partition_broadcast(P)
                        .rearrange("p (a d) -> p a d", a=4)),
                       (subln[:, :], diff_subln[l].partition_broadcast(P)),
                       (qk_gain[:, :, :], qk_norm_gain[l].rearrange("a d -> (a d)").partition_broadcast(P)
                        .rearrange("p (a d) -> p a d", a=2)),
                       (bada[:, :], b_ada[l].rearrange("(j n) -> j n", n=512)),
                       (cache_a[:, 0, :], cache_a_k[0, l].rearrange("t h c d -> t (h c d)")),
                       (cache_a[:, 1, :], cache_a_v[0, l].rearrange("t h d -> t (h d)")),
                       (cache_b[:, 0, :], cache_b_k[0, l].rearrange("t h d -> t (h d)")),
                       (cache_b[:, 1, :], cache_b_v[0, l].rearrange("t h d -> t (h d)"))]
                for dst, s in src:
                    pool.dma_start(dst, s).then_inc(params_loaded, 16)

            def load_ln(l, which):
                pool.dma_start(ln_par[:, 0, :], ln_gain[l, which].partition_broadcast(P)).then_inc(ln_loaded, 16)
                pool.dma_start(ln_par[:, 1, :], ln_bias[l, which].partition_broadcast(P)).then_inc(ln_loaded, 16)

            pool.dma_start(cst[:, :], consts).then_inc(first_loaded, 16)
            pool.dma_start(cond_raw[:, 0, :], c_ctx.rearrange("(p k) -> p k", k=KD)).then_inc(first_loaded, 16)
            pool.dma_start(cond_raw[:, 1, :], c[0].rearrange("(p k) -> p k", k=KD)).then_inc(first_loaded, 16)
            pool.dma_start(x[:, 0, :], x_prompt[0]).then_inc(first_loaded, 16)
            pool.dma_start(x[:, 1:3, :], x_sample[0].rearrange("(i p) d -> p i d", p=P)).then_inc(first_loaded, 16)
            pool.dma_start(w_rt[:, :, :], w_router[0].rearrange("(k p) e -> p k e", p=P)).then_inc(router_loaded, 16)
            for l in range(DEPTH):
                if l:
                    pool.wait_ge(x_ready, 6)
                load_params(l)
                rstds(3, 8)
                rstds(3, 2)
                pool.wait_ge(post_done, 10 * l + 10)
                pool.wait_ge(qkv_copied, 15 * l + 15)
                pool.dma_start(new_a_k[0, l].rearrange("t h c d -> t (h c d)"), qkv[:, 0, AK:AV]).then_inc(stored, 16)
                pool.dma_start(new_a_v[0, l].rearrange("t h d -> t (h d)"), qkv[:, 0, AV:BQ]).then_inc(stored, 16)
                pool.dma_start(new_b_k[0, l].rearrange("t h d -> t (h d)"), qkv[:, 0, BK:BV]).then_inc(stored, 16)
                pool.dma_start(new_b_v[0, l].rearrange("t h d -> t (h d)"), qkv[:, 0, BV:COLS]).then_inc(stored, 16)
                rstds(3, 4)
                pool.wait_ge(oT_mm, 6 * l + 6)
                load_ln(l, 0)
                rstds(3, 1)
                pool.wait_ge(x_ready, 6 * l + 3)
                load_ln(l, 1)
                rstds(3, 1)
            pool.wait_ge(x_ready, 12)
            pool.dma_start(y_prompt[0], x[:, 0, :]).then_inc(stored, 16)
            pool.dma_start(y_sample[0].rearrange("(i p) d -> p i d", p=P), x[:, 1:3, :]).then_inc(stored, 16)
            pool.wait_ge(stored, 16 * (4 * DEPTH + 2))

        @block.scalar
        def _(act):
            def copy_ada_row(l, j):
                a = 12 * l + j
                act.wait_ge(ada_mm, a + 1)
                if j >= 10:
                    dst = gate2_rows[:, j - 10, :]
                    if l:
                        act.wait_ge(ada_expanded, 16)
                else:
                    dst = ada_row[:, :]
                    if a:
                        act.wait_ge(ada_expanded, 16 * l + ada_expands_before(j))
                act.activation(dst, ps[0:2, 7, :], ACT.Copy).then_inc(ada_row_copied, 1)

            def modulate(l, which):
                h = 2 * l + which
                for kc in range(0, KD, 2):
                    act.wait_ge(xT_mm, 8 * h + kc + 1)
                    act.wait_ge(ada_exp_copied, 16 * l + (16 if which else 4))
                    b = 4 + kc % 2
                    act.activation(hT[:, kc, 0:P], ps[:, b, 0:P], ACT.Identity,
                                   bias=mod[:, 2 * which, kc, 0:1], scale=mod[:, 2 * which + 1, kc, 0:1])
                    act.activation(hT[:, kc, P:TOKENS], ps[:, b, P:TOKENS], ACT.Identity,
                                   bias=mod[:, 2 * which, kc, 1:2],
                                   scale=mod[:, 2 * which + 1, kc, 1:2]).then_inc(hT_act, 1)

            def copy_qkv(l, n):
                c0, w = PIECE_COLS[n]
                for i in range(NT):
                    q = 15 * l + 3 * n + i
                    act.wait_ge(qkv_mm, q + 1)
                    dst, src = qkv[:, i, c0:c0 + w], ps[:, (3 * n + i) % 4, 0:w]
                    if n == 3:
                        dst = dst.rearrange("p (h g d) -> p g h d", g=GKV, d=HD)
                        src = src.rearrange("p (g h d) -> p g h d", g=GKV, d=HD)
                    act.activation(dst, src, ACT.Copy).then_inc(qkv_copied, 1)

            def copy_qt(l, gs):
                for g in gs:
                    n, i = GROUPS[g]
                    act.wait_ge(qt_mm, NGROUPS * l + g + 1)
                    t0 = P * i
                    dst = {0: qT[:, 0:4, t0:t0 + P], 1: kT[:, 0:4, t0:t0 + P], 3: qT[:, 4:8, t0:t0 + P],
                           4: kT[:, 4:5, t0:t0 + P], "ca": kT[:, 0:4, TOKENS:TOKENS + P],
                           "cb": kT[:, 4:5, TOKENS:TOKENS + P]}[n]
                    m = dst.shape[1]
                    act.activation(dst, ps[:, 4 + g % 4, 0:P * m].rearrange("p (h t) -> p h t", h=m),
                                   ACT.Copy).then_inc(qt_copied, 1)

            def exps(l, v):
                u = UNITS * l + v
                i, _ = tile_of_unit(v)
                nk = P if i == 0 else 3 * P
                act.wait_ge(max_done, u + 1)
                if v >= 2:
                    act.wait_ge(pT_mm, u - 1)
                for cc in range(2):
                    ins = act.activation(prob[:, v % 2, cc, 0:nk], ps[:, 2 * (v % 2) + cc, 0:nk], ACT.Exp,
                                         bias=nbias[:, v % 2, cc:cc + 1], scale=SCALE,
                                         accum_out=rsum[:, v % 4, cc:cc + 1])
                ins.then_inc(exp_done, 1)

            def copy_pT(l, v):
                u = UNITS * l + v
                i, pr = tile_of_unit(v)
                nk = P if i == 0 else 3 * P
                act.wait_ge(pT_mm, u + 1)
                if v >= 2:
                    act.wait_ge(o_mm, u - 1)
                cc = 1 if pr >= 4 else 0
                act.activation(pT[:, v % 2, cc, 0:nk], ps[:, 4 + cc, 0:nk], ACT.Copy).then_inc(pT_act, 1)

            def copy_hiddenT(s, k, w):
                act.wait_ge(hidT_mm, s + 1)
                act.activation(hidT[:, k % 2, :, :].rearrange("p f t -> p (f t)")[:, 0:w],
                               ps[:, 6 + k % 2, 0:w], ACT.Copy).then_inc(hidT_copied, 1)

            def silu(s, k, w):
                act.wait_ge(gu_mm, s + 1)
                act.activation(sil[:, k % 2, 0:w], ps[:, 6 + k % 2, 0:w], ACT.Silu).then_inc(sil_ready, 1)

            act.wait_ge(first_loaded, 80)
            act.activation(cond[:, :, :], cond_raw[:, :, :].rearrange("p a k -> p k a"), ACT.Silu).then_inc(silu_done, 1)
            for l in range(DEPTH):
                for j in range(4):
                    copy_ada_row(l, j)
                modulate(l, 0)
                act.wait_ge(params_loaded, 128 * (l + 1))
                act.wait_ge(lam_sums, l + 1)
                act.activation(lam_exp[:, :], lam_sum[:, :], ACT.Exp).then_inc(lam_exps, 1)
                if l:
                    act.wait_ge(stored, 64)
                copy_qkv(l, 0)
                copy_qkv(l, 1)
                copy_qt(l, range(0, 3))
                copy_qkv(l, 2)
                copy_qt(l, range(3, 6))
                copy_qkv(l, 3)
                copy_qt(l, range(6, 8))
                copy_qkv(l, 4)
                copy_qt(l, range(8, 14))
                for v in range(UNITS + 1):
                    if v < UNITS:
                        exps(l, v)
                    if v % 3 == 1:
                        copy_ada_row(l, 4 + v // 3)
                    if v >= 1:
                        copy_pT(l, v - 1)
                for i in range(NT):
                    for hf in range(2):
                        act.wait_ge(oT_mm, 6 * l + 2 * i + hf + 1)
                        act.activation(hT[:, 4 * hf:4 * hf + 4, P * i:P * i + P],
                                       ps[:, 2 * i + hf, :].rearrange("p (k t) -> p k t", k=4),
                                       ACT.Copy).then_inc(oT_copied, 1)
                modulate(l, 1)
                if l == 0:
                    for s in range(DENSE + 1):
                        if s:
                            copy_hiddenT(s - 1, s - 1, FC)
                        if s < DENSE:
                            silu(s, s, FC)
            for k in range(6):
                act.wait_ge(hTok_mm, k + 1)
                act.activation(h_tok[:, k // 2, 512 * (k % 2):512 * (k % 2) + 512], ps[:, 1 + k, :],
                               ACT.Copy).then_inc(hTok_copied, 1)
            act.wait_ge(top_ready, 1)
            act.activation(expo[:, :, :], expo[:, :, :], ACT.Exp).then_inc(expo_ready, 1)
            act.wait_ge(sched_ready, 1)

            def gathered(nb, b0):
                def rows(b):
                    act.wait_ge(xg_rows_mm, b0 + (b + 1))
                    act.activation(xg_rows[:, b % 2, :], ps[:, 6 + b % 2, :], ACT.Copy).then_inc(xg_rows_copied, 1)

                def turned(b):
                    act.wait_ge(xgT_mm, b0 + (b + 1))
                    act.activation(hT[:, :, BT * b:BT * b + BT].rearrange("p (n m) t -> p m n t", n=2),
                                   ps[:, 6 + b % 2, :].rearrange("p (m n t) -> p m n t", m=4, n=2),
                                   ACT.Copy).then_inc(xgT_copied, 1)

                def rest(b):
                    if b + 1 < MAX_BLOCKS:
                        with act.If(nb > b + 1):
                            rows(b + 1)
                            turned(b)
                            rest(b + 1)
                        with act.Else():
                            turned(b)
                    else:
                        turned(b)

                rows(0)
                rest(0)

            nb0 = act.value_load(sched[0:1, 0:1], min_val=1, max_val=MAX_BLOCKS)
            gathered(nb0, 0)
            with act.Fori(0, NE) as t:
                nb = act.value_load(sched[0:1, bass.ds(t, 1)], min_val=1, max_val=MAX_BLOCKS)
                b0 = act.value_load(sched[0:1, bass.ds(t + (NE + 1), 1)], min_val=0, max_val=MAX_BLOCKS * NE)
                for ch in range(NCH):
                    s0 = b0 * NCH + nb * ch + DENSE

                    def rest(b):
                        copy_hiddenT(s0 + b, b, P)
                        if b + 1 < MAX_BLOCKS:
                            with act.If(nb > b + 1):
                                silu(s0 + (b + 1), b + 1, P)
                                rest(b + 1)

                    silu(s0, 0, P)
                    rest(0)
                act.wait_ge(chunk_done, t * NCH + 2 * NCH)

                def copy_y(b):
                    for h in range(2):
                        lo = BT * h
                        ins = act.activation(y_sb[lo:lo + BT, b // 2, (h + b) % 2, :], ps[lo:lo + BT, b, :], ACT.Copy)
                    ins.then_inc(y_copied, 1)

                each_block(act, nb, copy_y)
                nb_next = act.value_load(sched[0:1, bass.ds(t + 1, 1)], min_val=1, max_val=MAX_BLOCKS)
                gathered(nb_next, b0 + nb)

        @block.vector
        def _(dve):
            chain = [0]
            n_rstd = [0]

            def link(ins):
                chain[0] += 1
                ins.then_inc(dve_step, 1)
                dve.wait_ge(dve_step, chain[0])

            def rstd_of(width, mean_scale, src):
                dve.tensor_scalar(var_in[:, 0:width], src, mean_scale, EPS, ALU.mult, ALU.add).then_inc(var_ready, 1)
                n_rstd[0] += 1
                dve.wait_ge(rstd_ready, n_rstd[0])

            def copy_expansion(l, k):
                dve.wait_ge(ada_expanded, 16 * l + k + 1)
                if k < 4 or 8 <= k < 12:
                    j = k if k < 4 else k - 2
                    s = j // 2 if j < 4 else j // 2 - 1
                    dst = mod[:, s, 4 * (j % 2):4 * (j % 2) + 4, :]
                    ins = dve.tensor_scalar(dst, ps[:, 7, 0:8].rearrange("p (k a) -> p k a", a=2),
                                            float(s % 2), None, ALU.add)
                else:
                    k4 = k % 4
                    ins = dve.tensor_copy(gate[:, k4 % 2, 512 * (k4 // 2):512 * (k4 // 2) + 512], ps[:, 7, :])
                ins.then_inc(ada_exp_copied, 1)

            def modulate(l, which):
                h = 2 * l + which
                dve.wait_ge(ada_exp_copied, 16 * l + (16 if which else 4))
                for kc in range(1, KD, 2):
                    dve.wait_ge(xT_mm, 8 * h + kc + 1)
                    b = 4 + kc % 2
                    dve.tensor_scalar(hT[:, kc, 0:P], ps[:, b, 0:P], mod[:, 2 * which + 1, kc, 0:1],
                                      mod[:, 2 * which, kc, 0:1], ALU.mult, ALU.add)
                    dve.tensor_scalar(hT[:, kc, P:TOKENS], ps[:, b, P:TOKENS], mod[:, 2 * which + 1, kc, 1:2],
                                      mod[:, 2 * which, kc, 1:2], ALU.mult, ALU.add).then_inc(hT_dve, 1)

            def rope(i, c0, heads):
                w = heads * HD
                v = qkv[:, i, c0:c0 + w].rearrange("p (h d) -> p h d", d=HD)
                v4 = qkv[:, i, c0:c0 + w].rearrange("p (h a s d) -> p h a s d", a=2, s=2, d=16)
                ta = rope_a[:, 0:w].rearrange("p (h d) -> p h d", d=HD)
                tb = rope_b[:, 0:w].rearrange("p (h a s d) -> p h a s d", a=2, s=2, d=16)
                cos = cst[:, C_COS + HD * (i - 1):C_COS + HD * i].unsqueeze(1).broadcast_to([P, heads, HD])
                sin = cst[:, C_SIN + HD * (i - 1):C_SIN + HD * i].rearrange("p (a s d) -> p a s d", a=2, s=2)
                dve.tensor_tensor(ta, v, cos, ALU.mult)
                for s in range(2):
                    ins = dve.tensor_tensor(
                        tb[:, :, :, s, :], v4[:, :, :, 1 - s, :],
                        sin[:, :, s, :].unsqueeze(1).broadcast_to([P, heads, 2, 16]), ALU.mult)
                link(ins)
                return dve.tensor_tensor(v, ta, rope_b[:, 0:w].rearrange("p (h d) -> p h d", d=HD), ALU.add)

            def head_norm(v, heads, width, gain, extra):
                sq = rope_a[:, 0:heads * width].rearrange("p (h d) -> p h d", d=width)
                link(dve.tensor_tensor(sq, v, v, ALU.mult))
                link(dve.tensor_reduce(var_in[:, 0:heads], sq, AX, ALU.add))
                rstd_of(heads, 1.0 / width, var_in[:, 0:heads])
                link(dve.tensor_tensor(v, v, rstd[:, 0:heads].unsqueeze(2).broadcast_to([P, heads, width]), ALU.mult))
                return dve.scalar_tensor_tensor(out=v, in0=v, scalar=extra,
                                                in1=gain.unsqueeze(1).broadcast_to([P, heads, width]),
                                                op0=ALU.mult, op1=ALU.mult)

            def post(l, n, i):
                dve.wait_ge(qkv_copied, 15 * l + 3 * n + i + 1)
                c0 = {0: AQ, 1: AK, 3: BQ, 4: BK}[n]
                heads = {0: 8, 1: 8, 3: GH, 4: GKV}[n]
                ins = None
                if n >= 3:
                    v = qkv[:, i, c0:c0 + heads * HD].rearrange("p (h d) -> p h d", d=HD)
                    ins = head_norm(v, heads, HD, qk_gain[:, n - 3, :], 1.0)
                    if i:
                        link(ins)
                if i:
                    ins = rope(i, c0, heads)
                ins.then_inc(post_done, 1)
                dve.wait_ge(post_done, 10 * l + POSTS.index((n, i)) + 1)

            def lam(l):
                dve.wait_ge(params_loaded, 128 * (l + 1))
                for a in range(2):
                    ins = dve.tensor_tensor(lam_tmp[:, a, :], lam_in[:, 2 * a, :], lam_in[:, 2 * a + 1, :], ALU.mult)
                link(ins)
                dve.tensor_reduce(lam_sum[:, :], lam_tmp[:, :, :], AX, ALU.add).then_inc(lam_sums, 1)
                dve.wait_ge(lam_exps, l + 1)
                lam_init = 0.8 - 0.6 * math.exp(-0.3 * l)
                link(dve.tensor_tensor(neg_lam[:, :], lam_exp[:, 1:2], lam_exp[:, 0:1], ALU.subtract))
                link(dve.tensor_scalar(neg_lam[:, :], neg_lam[:, :], -lam_init, None, ALU.add))

            def row_max(l, v):
                u = UNITS * l + v
                i, _ = tile_of_unit(v)
                nk = P if i == 0 else 3 * P
                dve.wait_ge(s_mm, u + 1)
                b = 2 * (v % 2)
                link(dve.tensor_reduce(smax[:, v % 2, :], ps[:, b:b + 2, 0:nk], AX, ALU.max))
                dve.tensor_scalar(nbias[:, v % 2, :], smax[:, v % 2, :], -SCALE, None, ALU.mult).then_inc(max_done, 1)

            def combine(l, v):
                u = UNITS * l + v
                i, pr = tile_of_unit(v)
                nk = P if i == 0 else 3 * P
                dve.wait_ge(exp_done, u + 1)
                ins = dve.reciprocal(rinv[:, v % 4, :], rsum[:, v % 4, :])
                if pr < 4:
                    link(ins)
                    link(dve.tensor_tensor(rlam[:, :], rinv[:, v % 4, 1:2], neg_lam[:, :], ALU.mult))
                    p1, p0 = prob[:, v % 2, 1, 0:nk], prob[:, v % 2, 0, 0:nk]
                    link(dve.tensor_scalar(p1, p1, rlam[:, 0:1], None, ALU.mult))
                    ins = dve.scalar_tensor_tensor(out=p0, in0=p0, scalar=rinv[:, v % 4, 0:1], in1=p1,
                                                   op0=ALU.mult, op1=ALU.add)
                ins.then_inc(soft_done, 1)

            def copy_pT(l, v):
                u = UNITS * l + v
                i, pr = tile_of_unit(v)
                nk = P if i == 0 else 3 * P
                if pr >= 4:
                    dve.wait_ge(pT_mm, u + 1)
                    dve.tensor_copy(pT[:, v % 2, 0, 0:nk], ps[:, 4, 0:nk]).then_inc(pT_dve, 1)

            def copy_o(l, v):
                u = UNITS * l + v
                i, pr = tile_of_unit(v)
                dve.wait_ge(o_mm, u + 1)
                if pr < 4:
                    dve.tensor_copy(o[:, i, P * pr:P * pr + P], ps[:, 6, 0:P]).then_inc(o_copied, 1)
                    if pr == 3:
                        dve.wait_ge(o_copied, u + 1)
                        lam_init = 0.8 - 0.6 * math.exp(-0.3 * l)
                        v3 = o[:, i, 0:DW].rearrange("p (h d) -> p h d", d=2 * HD)
                        sq = squares[:, 0:DW].rearrange("p (h d) -> p h d", d=2 * HD)
                        link(dve.tensor_tensor(sq, v3, v3, ALU.mult))
                        link(dve.tensor_reduce(var_in[:, 0:DH], sq, AX, ALU.add))
                        rstd_of(DH, 1.0 / (2 * HD), var_in[:, 0:DH])
                        link(dve.tensor_tensor(v3, v3, rstd[:, 0:DH].unsqueeze(2).broadcast_to([P, DH, 2 * HD]),
                                               ALU.mult))
                        link(dve.scalar_tensor_tensor(out=v3, in0=v3, scalar=1.0 - lam_init,
                                                      in1=subln[:, :].unsqueeze(1).broadcast_to([P, DH, 2 * HD]),
                                                      op0=ALU.mult, op1=ALU.mult))
                else:
                    for cc in range(2):
                        hq = pr - 4 + 4 * cc
                        ins = dve.tensor_scalar(o[:, i, DW + HD * hq:DW + HD * hq + HD],
                                                ps[:, 6, HD * cc:HD * cc + HD],
                                                rinv[:, v % 4, cc:cc + 1], None, ALU.mult)
                    ins.then_inc(o_copied, 1)

            def residual(l, which, source, waits):
                e = 2 * l + which
                dve.wait_ge(ln_loaded, 32 * (e + 1))
                for i in range(NT):
                    waits(i)
                    cd = 0 if i == 0 else 1
                    link(dve.tensor_tensor(mixed.rearrange("p (a n) -> p a n", a=2), source(i),
                                           gate[:, cd, :].rearrange("p (a n) -> p a n", a=2), ALU.mult))
                    link(dve.scalar_tensor_tensor(out=x[:, i, :], in0=x[:, i, :], scalar=ALPHA, in1=mixed,
                                                  op0=ALU.mult, op1=ALU.add))
                    for a in range(2):
                        ins = dve.bn_stats(stats[:, a, :], x[:, i, 512 * a:512 * a + 512])
                    link(ins)
                    link(dve.bn_aggr(mv[:, :], stats[:, :, :]))
                    rstd_of(1, 1.0, mv[:, 1:2])
                    link(dve.tensor_scalar(x[:, i, :], x[:, i, :], mv[:, 0:1], rstd[:, 0:1],
                                           ALU.subtract, ALU.mult))
                    link(dve.tensor_tensor(x[:, i, :], x[:, i, :], ln_par[:, 0, :], ALU.mult))
                    dve.tensor_tensor(x[:, i, :], x[:, i, :], ln_par[:, 1, :], ALU.add).then_inc(x_ready, 1)
                    dve.wait_ge(x_ready, 3 * e + i + 1)

            def ffn_mul(s, k, w):
                dve.wait_ge(sil_ready, s + 1)
                dve.tensor_tensor(hid[:, k % 2, 0:w], sil[:, k % 2, 0:w], ps[:, 6 + k % 2, w:2 * w],
                                  ALU.mult).then_inc(hid_ready, 1)

            link(dve.memset(neg_half[:, :], -0.5))
            link(dve.memset(var_in[:, :], 1.0))
            dve.wait_ge(first_loaded, 80)
            for l in range(DEPTH):
                for k in range(4):
                    copy_expansion(l, k)
                modulate(l, 0)
                lam(l)
                for n, i in POSTS:
                    post(l, n, i)
                for v in range(UNITS + 3):
                    if v < UNITS:
                        row_max(l, v)
                    if 2 <= v < UNITS + 2:
                        copy_pT(l, v - 2)
                    if 1 <= v <= UNITS:
                        combine(l, v - 1)
                    if v >= 3:
                        copy_o(l, v - 3)
                    q, r = divmod(v, 3)
                    if q < 8 and r == 2:
                        for k in EXPAND_OF[4 + q]:
                            copy_expansion(l, k)
                residual(l, 0, lambda i: ps[:, 2 * i:2 * i + 2, :],
                         lambda i: dve.wait_ge(out_mm, 6 * l + 3 + i + 1))
                for k in range(12, 16):
                    copy_expansion(l, k)
                modulate(l, 1)
                if l == 0:
                    for s in range(DENSE):
                        ffn_mul(s, s, FC)
                    residual(l, 1, lambda i: ps[:, 2 * i:2 * i + 2, :],
                             lambda i: dve.wait_ge(chunk_done, NCH))

            dve.wait_ge(logit_mm, 1)
            link(dve.tensor_copy(logit[:, :, :], ps[:, 0, 0:NT * NE].rearrange("p (i e) -> p i e", i=NT)))
            link(dve.tensor_reduce(top[:, :], logit[:, :, :], AX, ALU.max))
            dve.tensor_tensor(expo[:, :, :], logit[:, :, :], top[:, :].unsqueeze(2).broadcast_to([P, NT, NE]),
                              ALU.subtract).then_inc(top_ready, 1)
            pr3 = pair[:, :].rearrange("p (i e f) -> p i e f", i=NT, e=NE)
            pr4 = pair2[:, :].rearrange("p (i e f) -> p i e f", i=NT, e=NE)
            for i in range(NT):
                other = logit[:, i, :].unsqueeze(1).broadcast_to([P, NE, NE])
                own = logit[:, i, :].unsqueeze(2).broadcast_to([P, NE, NE])
                dve.tensor_tensor(pr3[:, i], other, own, ALU.is_gt)
                ins = dve.tensor_tensor(pr4[:, i], other, own, ALU.is_equal)
            link(ins)
            low = cst[:, C_LOW:C_LOW + 64]
            link(dve.tensor_tensor(pair2[:, :].rearrange("p (i q) -> p i q", i=NT),
                                   pair2[:, :].rearrange("p (i q) -> p i q", i=NT),
                                   low.unsqueeze(1).broadcast_to([P, NT, 64]), ALU.mult))
            link(dve.tensor_tensor(pair[:, :], pair[:, :], pair2[:, :], ALU.add))
            link(dve.tensor_reduce(place[:, :, :].rearrange("p i e -> p (i e)"),
                                   pair[:, :].rearrange("p (q f) -> p q f", f=NE), AX, ALU.add))
            dve.tensor_scalar(chosen[:, :, :], place[:, :, :], 1.5, None, ALU.is_lt).then_inc(chosen_ready, 1)
            dve.wait_ge(chosen_ready, 1)
            dve.wait_ge(expo_ready, 1)
            link(dve.tensor_tensor(gates[:, :, :], expo[:, :, :], chosen[:, :, :], ALU.mult))
            link(dve.tensor_reduce(gsum[:, :], gates[:, :, :], AX, ALU.add))
            link(dve.reciprocal(gsum[:, :], gsum[:, :]))
            link(dve.tensor_tensor(gates[:, :, :], gates[:, :, :], gsum[:, :].unsqueeze(2).broadcast_to([P, NT, NE]),
                                   ALU.mult))
            dve.wait_ge(prefix_mm, 1)
            ranks = rank[:, :, 0:NE]
            link(dve.memset(rank[:, :, :], 0.0))
            link(dve.tensor_scalar(ranks, ps[:, 0, 32:32 + NT * NE].rearrange("p (i e) -> p i e", i=NT),
                                   10000.0, None, ALU.add))
            link(dve.tensor_tensor(ranks, ranks, chosen[:, :, :], ALU.mult))
            link(dve.tensor_scalar(rank[:, :, :], rank[:, :, :], -10000.0, None, ALU.add))
            link(dve.tensor_copy(counts[:, :], ps[:, 0, 64:64 + NE]))
            link(dve.memset(blocks[:, NE:NE + 1], 1.0))
            nblk = blocks[:, 0:NE]
            link(dve.tensor_scalar(nblk, counts[:, :], BT + 0.5, 1.0, ALU.is_gt, ALU.add))
            for b in range(2, MAX_BLOCKS):
                link(dve.scalar_tensor_tensor(out=nblk, in0=counts[:, :], scalar=BT * b + 0.5,
                                              in1=nblk, op0=ALU.is_gt, op1=ALU.add))
            low3 = pair[:, 0:64].rearrange("p (e f) -> p e f", e=NE)
            link(dve.tensor_tensor(low3, nblk.unsqueeze(1).broadcast_to([P, NE, NE]),
                                   low.rearrange("p (e f) -> p e f", e=NE), ALU.mult))
            link(dve.tensor_reduce(cum[:, 0:NE], low3, AX, ALU.add))
            link(dve.tensor_reduce(cum[:, NE:NE + 1], nblk, AX, ALU.add))
            link(dve.tensor_scalar(pairs[:, :], counts[:, :], 2 * BT + 0.5, 1.0, ALU.is_gt, ALU.add))
            link(dve.scalar_tensor_tensor(out=pairs[:, :], in0=counts[:, :], scalar=4 * BT + 0.5,
                                          in1=pairs[:, :], op0=ALU.is_gt, op1=ALU.add))
            link(dve.tensor_tensor(low3, pairs[:, :].unsqueeze(1).broadcast_to([P, NE, NE]),
                                   low.rearrange("p (e f) -> p e f", e=NE), ALU.mult))
            link(dve.tensor_reduce(pair_cum[:, :], low3, AX, ALU.add))
            dve.memset(y_acc[:, :, :], 0.0).then_inc(spread_added, 1)
            dve.memset(y_sb[:, :, :, :], 0.0)
            dve.tensor_copy(sched[:, 2 * NE + 2:3 * NE + 2], pair_cum[:, :])
            link(dve.tensor_copy(sched[:, 0:NE + 1], blocks[:, :]))
            dve.tensor_copy(sched[:, NE + 1:2 * NE + 2], cum[:, :]).then_inc(sched_ready, 1)
            dve.wait_ge(sched_ready, 1)

            def select(e):
                for i in range(NT):
                    ins = dve.tensor_scalar(pick[:, i, :], cst[:, C_IOTA:C_IOTA + TOKENS], rank[:, i, e], None,
                                            ALU.is_equal)
                ins.then_inc(pick_ready, 1)

            select(slice(0, 1))
            with dve.Fori(0, NE) as t:
                nb = dve.value_load(sched[0:1, bass.ds(t, 1)], min_val=1, max_val=MAX_BLOCKS)
                b0 = dve.value_load(sched[0:1, bass.ds(t + (NE + 1), 1)], min_val=0, max_val=MAX_BLOCKS * NE)
                p0 = dve.value_load(sched[0:1, bass.ds(t + (2 * NE + 2), 1)], min_val=0, max_val=MAX_PAIRS * NE)

                def select_gates(b):
                    if b >= 2:
                        dve.wait_ge(pgT_mm, p0 + (b - 1))
                    for i in range(NT):
                        ins = dve.tensor_scalar(pick_g[:, b % 2, i, :], cst[:, C_IOTA + P * b:C_IOTA + P * b + P],
                                                rank[:, i, bass.ds(t, 1)], gates[:, i, bass.ds(t, 1)],
                                                ALU.is_equal, ALU.mult)
                    ins.then_inc(pick_g_ready, 1)

                def copy_gates(b):
                    dve.wait_ge(pgT_mm, p0 + (b + 1))
                    for n in range(2):
                        ins = dve.tensor_copy(pick_gT[:, b, n, :, :],
                                              ps[:, 6 + n, 0:NT * P].rearrange("p (i t) -> p i t", i=NT))
                    ins.then_inc(pgT_copied, 1)

                def copy_gates_from(b):
                    copy_gates(b)
                    if b + 1 < MAX_PAIRS:
                        with dve.If(nb > 2 * b + 2):
                            if b == 0:
                                with dve.If(nb > 4):
                                    select_gates(2)
                            copy_gates_from(b + 1)

                for ch in range(NCH):
                    s0 = b0 * NCH + nb * ch + DENSE
                    each_block(dve, nb, lambda b: ffn_mul(s0 + b, b, P))
                    if ch == 0:
                        select(bass.ds(t + 1, 1))
                        select_gates(0)
                        with dve.If(nb > 2):
                            select_gates(1)
                copy_gates_from(0)
                dve.wait_ge(spread_added, t * 6 + 1)
                for k in range(6):
                    dve.wait_ge(spread_mm, t * 6 + (k + 1))
                    ya = y_acc[:, k // 2, 512 * (k % 2):512 * (k % 2) + 512]
                    dve.tensor_tensor(ya, ya, ps[:, k, :], ALU.add).then_inc(spread_added, 1)
            dve.wait_ge(spread_added, 6 * NE + 1)
            residual(1, 1, lambda i: y_acc[:, i, :].rearrange("p (a n) -> p a n", a=2), lambda i: None)

        @block.tensor
        def _(pe):
            def ada_rows(l, j, k):
                a = 12 * l + j
                pe.wait_ge(gu_landed[gu_slot[k]], gu_value[k])
                if a:
                    pe.wait_ge(ada_row_copied, a)
                    pe.wait_ge(ada_exp_copied, 16 * l + ada_expands_before(j))
                w = piece_view(k)
                for kc in range(KD):
                    pe.matmul(ps[0:2, 7, :], cond[:, kc, :], w[:, kc, :], start=(kc == 0), stop=False)
                pe.matmul(ps[0:2, 7, :], cst[0:12, C_PIECE + 2 * j:C_PIECE + 2 * j + 2], bada[:, :],
                          start=False, stop=True).then_inc(ada_mm, 1)

            def ada_expand(l, k):
                if k < 4 or 8 <= k < 12:
                    j = k if k < 4 else k - 2
                    pe.wait_ge(ada_row_copied, 12 * l + j + 1)
                    for q in range(4):
                        ins = pe.transpose(ps[:, 7, 2 * q:2 * q + 2], ada_row[:, P * q:P * q + P],
                                           cst[0:2, C_ID:C_ID + 2])
                else:
                    half, cd = k % 4 // 2, k % 2
                    if k < 8:
                        pe.wait_ge(ada_row_copied, 12 * l + 4 + half + 1)
                        row = ada_row[:, :]
                    else:
                        pe.wait_ge(ada_row_copied, 12 * l + 12)
                        row = gate2_rows[:, half, :]
                    pe.wait_ge(ada_exp_copied, 16 * l + k)
                    ins = pe.matmul(ps[:, 7, :], cst[0:2, C_SEL + P * cd:C_SEL + P * cd + P], row,
                                    start=True, stop=True)
                ins.then_inc(ada_expanded, 1)

            def turn_x(l, which):
                h = 2 * l + which
                if h:
                    pe.wait_ge(x_ready, 3 * h)
                for kc in range(KD):
                    if kc >= 2:
                        pe.wait_ge(hT_dve if kc % 2 else hT_act, 4 * h + kc // 2)
                    for i in range(NT):
                        ins = pe.transpose(ps[:, 4 + kc % 2, P * i:P * i + P], x[:, i, P * kc:P * kc + P], ident)
                    ins.then_inc(xT_mm, 1)
                pe.wait_ge(hT_act, 4 * h + 4)
                pe.wait_ge(hT_dve, 4 * h + 4)

            def project(l, n, k):
                w = PIECE_COLS[n][1]
                pe.wait_ge(gu_landed[gu_slot[k]], gu_value[k])
                v = piece_view(k, w)
                for i in range(NT):
                    q = 3 * n + i
                    if q >= 4:
                        pe.wait_ge(qkv_copied, 15 * l + q - 3)
                    for kc in range(KD):
                        ins = pe.matmul(ps[:, q % 4, 0:w], hT[:, kc, P * i:P * i + P], v[:, kc, :],
                                        start=(kc == 0), stop=(kc == KD - 1))
                    ins.then_inc(qkv_mm, 1)

            def turn_qk(l, gs):
                for g in gs:
                    n, i = GROUPS[g]
                    if (n, i) in POSTS:
                        pe.wait_ge(post_done, 10 * l + POSTS.index((n, i)) + 1)
                    elif n in (0, 1):
                        pe.wait_ge(qkv_copied, 15 * l + 3 * n + i + 1)
                    if g >= 4:
                        pe.wait_ge(qt_copied, NGROUPS * l + g - 3)
                    for m in range(1 if n in (4, "cb") else 4):
                        src = {0: qkv[:, i, AQ + P * m:AQ + P * m + P], 1: qkv[:, i, AK + P * m:AK + P * m + P],
                               3: qkv[:, i, BQ + P * m:BQ + P * m + P],
                               4: qkv[:, i, BK:BK + P], "ca": cache_a[:, 0, P * m:P * m + P],
                               "cb": cache_b[:, 0, :]}[n]
                        ins = pe.transpose(ps[:, 4 + g % 4, P * m:P * m + P], src, ident)
                    ins.then_inc(qt_mm, 1)

            def scores(l, v):
                u = UNITS * l + v
                i, pr = tile_of_unit(v)
                k0, nk = (0, P) if i == 0 else (P, 3 * P)
                if v >= 2:
                    pe.wait_ge(exp_done, u - 1)
                for cc in range(2):
                    ins = pe.matmul(ps[:, 2 * (v % 2) + cc, 0:nk], qT[HD * cc:HD * cc + HD, pr, P * i:P * i + P],
                                    kT[HD * cc:HD * cc + HD, min(pr, 4), k0:k0 + nk], start=True, stop=True)
                ins.then_inc(s_mm, 1)

            def turn_p(l, v):
                u = UNITS * l + v
                i, pr = tile_of_unit(v)
                pe.wait_ge(soft_done, u + 1)
                pe.wait_ge(pT_act, u)
                if gqa_before(u):
                    pe.wait_ge(pT_dve, gqa_before(u))
                for cc in range(1 if pr < 4 else 2):
                    for kb in range(1 if i == 0 else 3):
                        ins = pe.transpose(ps[:, 4 + cc, P * kb:P * kb + P],
                                           prob[:, v % 2, cc, P * kb:P * kb + P], ident)
                ins.then_inc(pT_mm, 1)

            def weigh_v(l, v):
                u = UNITS * l + v
                i, pr = tile_of_unit(v)
                pe.wait_ge(pT_act, u + 1)
                if pr >= 4:
                    pe.wait_ge(pT_dve, gqa_before(u) + 1)
                pe.wait_ge(o_copied, u)
                nb = 1 if i == 0 else 3
                for cc in range(1 if pr < 4 else 2):
                    for kb in range(nb):
                        if pr < 4:
                            c0, w = P * pr, P
                            rhs = (cache_a[:, 1, c0:c0 + w] if kb == 2 else
                                   qkv[:, 0 if i == 0 else kb + 1, AV + c0:AV + c0 + w])
                        else:
                            c0, w = HD * cc, HD
                            rhs = (cache_b[:, 1, c0:c0 + w] if kb == 2 else
                                   qkv[:, 0 if i == 0 else kb + 1, BV + c0:BV + c0 + w])
                        ins = pe.matmul(ps[:, 6, w * cc:w * cc + w], pT[:, v % 2, cc, P * kb:P * kb + P], rhs,
                                        start=(kb == 0), stop=(kb == nb - 1))
                ins.then_inc(o_mm, 1)

            def gate_up(s, k, w, lhs, half):
                b = 6 + k % 2
                for kc in range(4 * half, 4 * half + 4):
                    ins = pe.matmul(ps[:, b, :], lhs[kc], w[:, kc, :], start=(kc == 0), stop=(kc == KD - 1))
                if half:
                    ins.then_inc(gu_mm, 1)

            def turn_hidden(s, k):
                pe.wait_ge(hid_ready, s + 1)
                for f in range(2):
                    ins = pe.transpose(ps[:, 6 + k % 2, P * f:P * f + P], hid[:, k % 2, P * f:P * f + P], ident)
                ins.then_inc(hidT_mm, 1)

            def down(s, k, slot, bank, first, last):
                pe.wait_ge(hidT_copied, s + 1)
                wd = down_view(slot)
                for n in range(2):
                    for f in range(2):
                        ins = pe.matmul(ps[:, bank + n, :], hidT[:, k % 2, f, :], wd[:, f, 512 * n:512 * n + 512],
                                        start=(first and f == 0), stop=(last and f == 1))
                return ins

            pe.wait_ge(first_loaded, 80)
            pe.wait_ge(silu_done, 1)
            pe.wait_ge(params_loaded, 128)
            for l in range(DEPTH):
                k0 = first_gu[l]
                if l:
                    pe.wait_ge(params_loaded, 128 * (l + 1))
                    pe.wait_ge(x_ready, 6)
                for j in range(4):
                    ada_rows(l, j, k0 + j)
                    ada_expand(l, j)
                turn_x(l, 0)
                project(l, 0, k0 + 4)
                project(l, 1, k0 + 5)
                turn_qk(l, range(0, 3))
                project(l, 2, k0 + 6)
                turn_qk(l, range(3, 6))
                project(l, 3, k0 + 7)
                turn_qk(l, range(6, 8))
                project(l, 4, k0 + 8)
                turn_qk(l, range(8, 14))
                pe.wait_ge(qkv_copied, 15 * l + 15)
                pe.wait_ge(qt_copied, NGROUPS * (l + 1))
                for v in range(UNITS + 2):
                    if v < UNITS:
                        scores(l, v)
                    if 1 <= v <= UNITS:
                        turn_p(l, v - 1)
                    if v >= 2:
                        weigh_v(l, v - 2)
                    q, r = divmod(v, 3)
                    if q < 8 and r == 1:
                        ada_rows(l, 4 + q, k0 + 9 + q)
                    if q < 8 and r == 2:
                        for k in EXPAND_OF[4 + q]:
                            ada_expand(l, k)
                pe.wait_ge(o_copied, UNITS * (l + 1))
                for i in range(NT):
                    for hf in range(2):
                        for m in range(4):
                            ins = pe.transpose(ps[:, 2 * i + hf, P * m:P * m + P],
                                               o[:, i, P * (4 * hf + m):P * (4 * hf + m) + P], ident)
                        ins.then_inc(oT_mm, 1)
                pe.wait_ge(oT_copied, 6 * (l + 1))
                for n in range(2):
                    k = k0 + 17 + n
                    pe.wait_ge(gu_landed[gu_slot[k]], gu_value[k])
                    w = piece_view(k)
                    for i in range(NT):
                        for kc in range(KD):
                            ins = pe.matmul(ps[:, 2 * i + n, :], hT[:, kc, P * i:P * i + P], w[:, kc, :],
                                            start=(kc == 0), stop=(kc == KD - 1))
                        ins.then_inc(out_mm, 1)
                pe.wait_ge(x_ready, 6 * l + 3)
                for k in range(12, 16):
                    ada_expand(l, k)
                turn_x(l, 1)
                pe.wait_ge(ada_exp_copied, 16 * (l + 1))
                if l == 0:
                    for s in range(DENSE + 1):
                        ch, i = divmod(s, NT)
                        if s < DENSE:
                            k = dense_gu + ch
                            pe.wait_ge(gu_landed[gu_slot[k]], gu_value[k])
                            if s >= 2:
                                pe.wait_ge(hidT_copied, s - 1)
                            w = gu_ring[:, gu_slot[k], :].rearrange("p (k n) -> p k n", k=KD)
                            lhs = [hT[:, kc, P * i:P * i + P] for kc in range(KD)]
                            gate_up(s, s, w, lhs, 0)
                        if s:
                            turn_hidden(s - 1, s - 1)
                        if s < DENSE:
                            gate_up(s, s, w, lhs, 1)
                        if s:
                            pc, pi = divmod(s - 1, NT)
                            pe.wait_ge(d_landed[pc % D_SLOTS], 16 * (pc // D_SLOTS + 1))
                            ins = down(s - 1, s - 1, pc % D_SLOTS, 2 * pi, pc == 0, pc == NCH - 1)
                            if pi == NT - 1:
                                ins.then_inc(chunk_done, 1)

            pe.wait_ge(router_loaded, 16)
            for i in range(NT):
                for kc in range(KD):
                    ins = pe.matmul(ps[:, 0, NE * i:NE * i + NE], hT[:, kc, P * i:P * i + P], w_rt[:, kc, :],
                                    start=(kc == 0), stop=(kc == KD - 1))
            ins.then_inc(logit_mm, 1)
            for i in range(NT):
                for hf in range(2):
                    for m in range(4):
                        ins = pe.transpose(ps[:, 1 + 2 * i + hf, P * m:P * m + P],
                                           hT[:, 4 * hf + m, P * i:P * i + P], ident)
                    ins.then_inc(hTok_mm, 1)
            pe.wait_ge(chosen_ready, 1)
            for i in range(NT):
                for b in range(i):
                    pe.matmul(ps[:, 0, 32 + NE * i:32 + NE * i + NE], cst[:, C_ONES:C_ONES + P], chosen[:, b, :],
                              start=(b == 0), stop=False)
                pe.matmul(ps[:, 0, 32 + NE * i:32 + NE * i + NE], cst[:, C_UP:C_UP + P], chosen[:, i, :],
                          start=(i == 0), stop=True)
            for i in range(NT):
                ins = pe.matmul(ps[:, 0, 64:64 + NE], cst[:, C_ONES:C_ONES + P], chosen[:, i, :],
                                start=(i == 0), stop=(i == NT - 1))
            ins.then_inc(prefix_mm, 1)
            pe.wait_ge(hTok_copied, 6)
            pe.wait_ge(sched_ready, 1)

            def gather(nb, b0):
                def rows(b):
                    if b >= 2:
                        pe.wait_ge(xgT_copied, b0 + (b - 1))
                    for i in range(NT):
                        for n in range(2):
                            ins = pe.matmul(ps[BT * n:BT * n + BT, 6 + b % 2, :], pick[:, i, BT * b:BT * b + BT],
                                            h_tok[:, i, 512 * n:512 * n + 512], start=(i == 0), stop=(i == NT - 1))
                    ins.then_inc(xg_rows_mm, 1)

                def turn(b):
                    pe.wait_ge(xg_rows_copied, b0 + (b + 1))
                    for m in range(4):
                        ins = pe.transpose(ps[:, 6 + b % 2, P * m:P * m + P], xg_rows[:, b % 2, P * m:P * m + P], ident)
                    ins.then_inc(xgT_mm, 1)

                def rest(b):
                    if b + 1 < MAX_BLOCKS:
                        with pe.If(nb > b + 1):
                            rows(b + 1)
                            turn(b)
                            rest(b + 1)
                        with pe.Else():
                            turn(b)
                    else:
                        turn(b)

                rows(0)
                rest(0)

            nb0 = pe.value_load(sched[0:1, 0:1], min_val=1, max_val=MAX_BLOCKS)
            pe.wait_ge(pick_ready, 1)
            gather(nb0, 0)
            with pe.Fori(0, NE) as t:
                nb = pe.value_load(sched[0:1, bass.ds(t, 1)], min_val=1, max_val=MAX_BLOCKS)
                b0 = pe.value_load(sched[0:1, bass.ds(t + (NE + 1), 1)], min_val=0, max_val=MAX_BLOCKS * NE)
                p0 = pe.value_load(sched[0:1, bass.ds(t + (2 * NE + 2), 1)], min_val=0, max_val=MAX_PAIRS * NE)

                def gate_up_half(b, w, half):
                    for kc in range(4 * half, 4 * half + 4):
                        for f in range(2):
                            ins = pe.matmul(ps[BT * f:BT * f + BT, 6 + b % 2, 0:FC].rearrange("p (a f) -> p a f", a=2),
                                            hT[:, kc, BT * b:BT * b + BT], w[:, kc, :, P * f:P * f + P],
                                            start=(kc == 0), stop=(kc == KD - 1))
                    if half:
                        ins.then_inc(gu_mm, 1)

                def turn_half(s, b):
                    pe.wait_ge(hid_ready, s + 1)
                    pe.transpose(ps[:, 6 + b % 2, 0:P], hid[:, b % 2, 0:P], ident).then_inc(hidT_mm, 1)

                def down_half(s, b, wd, first, last):
                    pe.wait_ge(hidT_copied, s + 1)
                    if first and b == 0:
                        pe.wait_ge(spread_added, t * 6 + 1)
                    hT_flat = hidT[:, b % 2, :, :].rearrange("p f t -> p (f t)")
                    for f in range(2):
                        for n in range(2):
                            lo = BT * ((n + b) % 2)
                            ins = pe.matmul(ps[lo:lo + BT, b, :], hT_flat[:, BT * f:BT * f + BT],
                                            wd[:, f, 512 * n:512 * n + 512],
                                            start=(first and f == 0), stop=(last and f == 1))
                    return ins

                pe.wait_ge(xgT_copied, b0 + nb)
                for ch in range(NCH):
                    slot = ch % GU_SLOTS
                    pe.wait_ge(gu_landed[slot], t * (32 * GU_USES[slot]) + 32 * (gu_static[slot] + ch // 3 + 1))
                    pe.wait_ge(d_landed[slot], t * (16 * GU_USES[slot]) + 16 * (GU_USES[slot] + ch // 3 + 1))
                    w, wd = chunk_view(slot), down_view(slot)
                    s0 = b0 * NCH + nb * ch + DENSE
                    first, last = ch == 0, ch == NCH - 1

                    def rest(b):
                        if b + 1 < MAX_BLOCKS:
                            with pe.If(nb > b + 1):
                                gate_up_half(b + 1, w, 0)
                                turn_half(s0 + b, b)
                                gate_up_half(b + 1, w, 1)
                                down_half(s0 + b, b, wd, first, last)
                                rest(b + 1)
                            with pe.Else():
                                turn_half(s0 + b, b)
                                down_half(s0 + b, b, wd, first, last).then_inc(chunk_done, 1)
                        else:
                            turn_half(s0 + b, b)
                            down_half(s0 + b, b, wd, first, last).then_inc(chunk_done, 1)

                    gate_up_half(0, w, 0)
                    gate_up_half(0, w, 1)
                    rest(0)
                nb_next = pe.value_load(sched[0:1, bass.ds(t + 1, 1)], min_val=1, max_val=MAX_BLOCKS)
                pe.wait_ge(pick_ready, t + 2)
                gather(nb_next, b0 + nb)
                pe.wait_ge(xgT_copied, b0 + nb + nb_next)

                def turn_gates(b):
                    pe.wait_ge(pick_g_ready, p0 + (b + 1))
                    if b:
                        pe.wait_ge(pgT_copied, p0 + b)
                    for i in range(NT):
                        pe.transpose(ps[:, 6, P * i:P * i + P], pick_g[:, b % 2, i, :], ident)
                        for h in range(2):
                            ins = pe.matmul(ps[BT * h:BT * h + BT, 7, P * i:P * i + P],
                                            pick_g[:, b % 2, i, BT * (1 - h):BT * (1 - h) + BT], ident,
                                            start=True, stop=True)
                    ins.then_inc(pgT_mm, 1)

                def spread(b, last):
                    for k in range(6):
                        i, n = divmod(k, 2)
                        ins = pe.matmul(ps[:, k, :], pick_gT[:, b, n, i, :], y_sb[:, b, n, :],
                                        start=(b == 0), stop=last)
                        if last:
                            ins.then_inc(spread_mm, 1)

                def spread_from(b):
                    if b + 1 < MAX_PAIRS:
                        with pe.If(nb > 2 * b + 2):
                            turn_gates(b + 1)
                            spread(b, False)
                            spread_from(b + 1)
                        with pe.Else():
                            pe.wait_ge(pgT_copied, p0 + (b + 1))
                            spread(b, True)
                    else:
                        pe.wait_ge(pgT_copied, p0 + (b + 1))
                        spread(b, True)

                turn_gates(0)
                pe.wait_ge(y_copied, b0 + nb)
                spread_from(0)


EXPAND_OF = {4: [4, 5], 5: [6, 7], 6: [8], 7: [9], 8: [10], 9: [11], 10: [], 11: []}

_INS = ["x_prompt", "x_sample", "cache_a_k", "cache_a_v", "cache_b_k", "cache_b_v", "c", "c_ctx", "w_ada",
        "b_ada", "w_in", "w_out", "diff_lambda", "diff_subln", "qk_norm_gain", "ln_gain", "ln_bias",
        "w_ffn_gate", "w_ffn_up", "w_ffn_down", "w_router", "w_moe_gate", "w_moe_up", "w_moe_down"]
_OUTS = [(1, 128, 1024), (1, 256, 1024), (1, 2, 128, 4, 2, 64), (1, 2, 128, 4, 128),
         (1, 2, 128, 2, 64), (1, 2, 128, 2, 64)]


def kernel(**inputs):
    import concourse.bacc as bacc
    from concourse.bass_utils import run_bass_kernel_spmd

    nc = bacc.Bacc("TRN2", target_bir_lowering=False, num_devices=1)
    arrays, args = {}, []
    for name in _INS:
        arrays[f"in_{name}"] = np.ascontiguousarray(inputs[name])
    arrays["in_consts"] = shape_constants()
    for name, a in arrays.items():
        args.append(nc.dram_tensor(name, a.shape, mybir.dt.from_np(a.dtype), kind="ExternalInput").ap())
    for i, shape in enumerate(_OUTS):
        args.append(nc.dram_tensor(f"out_{i}", shape, F32, kind="ExternalOutput").ap())
    build(nc, *args)
    r = run_bass_kernel_spmd(nc, [arrays], core_ids=[0])
    return tuple(r.results[0][f"out_{i}"] for i in range(len(_OUTS)))
```

```python
import math
from contextlib import ExitStack

import numpy as np
import concourse.bass as bass
from concourse import mybir

F32 = mybir.dt.float32
F32R = mybir.dt.float32r
I32 = mybir.dt.int32
ALU = mybir.AluOpType
ACT = mybir.ActivationFunctionType
AX = mybir.AxisListType.X

P = 128
D = 1024
KD = D // P
DEPTH = 2
NT = 3
HD = 64
DH, GH, GKV = 4, 8, 2
DW = DH * 2 * HD
GW = GH * HD
KVW = GKV * HD
COLS = 3 * DW + GW + 2 * KVW
AQ, AK, AV, BQ, BK, BV = 0, DW, 2 * DW, 3 * DW, 3 * DW + GW, 3 * DW + GW + KVW
F = 2816
FC = 256
NCH = F // FC
NE = 8
GRID_W = 64
EPS = 1e-6
ALPHA = (2 * DEPTH) ** 0.25
SCALE = HD ** -0.5
TOKENS = NT * P
BT = 64
MAX_BLOCKS = TOKENS // BT
MAX_PAIRS = MAX_BLOCKS // 2
GU_SLOTS = 3
D_SLOTS = 3
GU_USES = [4, 4, 3]
UNITS = 24
NGROUPS = 14
POSTS = [(0, 1), (0, 2), (1, 1), (1, 2), (3, 0), (3, 1), (3, 2), (4, 0), (4, 1), (4, 2)]
GROUPS = [(0, 0), (0, 1), (0, 2), (1, 0), (1, 1), (1, 2), ("ca", 0), ("cb", 0),
          (3, 0), (3, 1), (3, 2), (4, 0), (4, 1), (4, 2)]
PIECE_COLS = [(0, 512), (512, 512), (1024, 512), (1536, 512), (2048, 256)]

C_ID, C_UP, C_ONES = 0, 128, 256
C_COS, C_SIN = 384, 512
C_SEL = 640
C_PIECE = 896
C_LOW = 920
C_IOTA = 984
C_END = C_IOTA + TOKENS


def shape_constants():
    c = np.zeros((P, C_END), np.float32)
    r = np.arange(P)
    c[:, C_ID:C_ID + P] = np.eye(P)
    c[:, C_UP:C_UP + P] = r[:, None] < r[None, :]
    c[:, C_IOTA:C_IOTA + TOKENS] = np.arange(TOKENS)
    c[:, C_ONES:C_ONES + P] = 1
    n_freq = HD // 4
    inv = np.float32(10000.0) ** (-np.arange(n_freq, dtype=np.float32) / n_freq)
    pos = np.arange(2 * P)
    ar = (pos // GRID_W).astype(np.float32)[:, None] * inv
    ac = (pos % GRID_W).astype(np.float32)[:, None] * inv
    ang = np.concatenate([ar, ar, ac, ac], axis=-1)
    sign = np.repeat(np.array([-1, 1, -1, 1], np.float32), n_freq)
    c[:, C_COS:C_COS + 2 * HD] = np.cos(ang).reshape(2, P, HD).transpose(1, 0, 2).reshape(P, -1)
    c[:, C_SIN:C_SIN + 2 * HD] = (np.sin(ang) * sign).reshape(2, P, HD).transpose(1, 0, 2).reshape(P, -1)
    for k in range(2):
        c[k, C_SEL + k * P:C_SEL + (k + 1) * P] = 1
    for j in range(12):
        c[j, C_PIECE + 2 * j:C_PIECE + 2 * j + 2] = 1
    e = np.arange(NE)
    c[:, C_LOW:C_LOW + 64] = (e[None, :] < e[:, None]).reshape(-1)
    return c


def tile_of_unit(v):
    return v // 8, v % 8


def gqa_before(u):
    return u // 8 * 4 + max(0, u % 8 - 4)


PROJ_HALVES = 14
WEIGHT_PARTS = PROJ_HALVES + 3 * NCH
ACT_PARTS = 8 + 6 + 8


def ada_expands_before(j):
    return [0, 1, 2, 3, 4, 6, 8, 9, 10, 11, 12, 12][j]


def build(nc, x_prompt, x_sample, cache_a_k, cache_a_v, cache_b_k, cache_b_v, c, c_ctx, w_ada,
          b_ada, w_in, w_out, diff_lambda, diff_subln, qk_norm_gain, ln_gain, ln_bias, w_ffn_gate,
          w_ffn_up, w_ffn_down, w_router, w_moe_gate, w_moe_up, w_moe_down, consts,
          y_prompt, y_sample, new_a_k, new_a_v, new_b_k, new_b_v):
    ctx = ExitStack()
    with ctx:
        def sb(name, shape, dt=F32):
            return ctx.enter_context(nc.sbuf_tensor(name, shape, dt))

        def sb_two(name, shape):
            with nc.sbuf_tensor(name, shape, F32) as values:
                pass
            return values, sb(name + "_parts", shape, F32R)

        def sem(name):
            return ctx.enter_context(nc.semaphore(name))

        gu_ring, gu_ring_parts = sb_two("gu_ring", [P, GU_SLOTS, KD * 512])
        d_ring, d_ring_parts = sb_two("d_ring", [P, D_SLOTS, 2 * D])
        cst = sb("cst", [P, C_END])
        x = sb("x", [P, NT, D])
        hT, hT_parts = sb_two("hT", [P, KD, TOKENS])
        qkv, qkv_parts = sb_two("qkv", [P, NT, COLS])
        scratch, scratch_parts = sb_two("scratch", [P, 8704])
        cache_a = sb("cache_a", [P, 2, DW])
        cache_b = sb("cache_b", [P, 2, KVW])
        o, o_parts = sb_two("o", [P, NT, D])
        gate = sb("gate", [P, 2, D])
        ada_row = sb("ada_row", [2, 512])
        gate2_rows = sb("gate2_rows", [2, 2, 512])
        mod = sb("mod", [P, 4, KD, 2])
        cond_raw = sb("cond_raw", [P, 2, KD])
        cond = sb("cond", [P, KD, 2])
        bada = sb("bada", [12, 512])
        lam_in = sb("lam_in", [P, 4, HD])
        lam_tmp = sb("lam_tmp", [P, 2, HD])
        lam_sum = sb("lam_sum", [P, 2])
        lam_exp = sb("lam_exp", [P, 2])
        neg_lam = sb("neg_lam", [P, 1])
        subln = sb("subln", [P, 2 * HD])
        qk_gain = sb("qk_gain", [P, 2, HD])
        smax = sb("smax", [P, 2, 2])
        nbias = sb("nbias", [P, 2, 2])
        rsum = sb("rsum", [P, 4, 2])
        rinv = sb("rinv", [P, 4, 2])
        rlam = sb("rlam", [P, 1])
        var_in = sb("var_in", [P, 8])
        rstd = sb("rstd", [P, 8])
        neg_half = sb("neg_half", [P, 8])
        stats = sb("stats", [P, 2, 6])
        mv = sb("mv", [P, 2])
        w_rt = sb("w_rt", [P, KD, NE])
        logit = sb("logit", [P, NT, NE])
        top = sb("top", [P, NT])
        expo = sb("expo", [P, NT, NE])
        pair = sb("pair", [P, NT * NE * NE])
        pair2 = sb("pair2", [P, NT * NE * NE])
        place = sb("place", [P, NT, NE])
        chosen = sb("chosen", [P, NT, NE])
        gates = sb("gates", [P, NT, NE])
        gsum = sb("gsum", [P, NT])
        rank = sb("rank", [P, NT, NE + 1])
        counts = sb("counts", [P, NE])
        blocks = sb("blocks", [P, NE + 1])
        cum = sb("cum", [P, NE + 1])
        pairs = sb("pairs", [P, NE])
        pair_cum = sb("pair_cum", [P, NE])
        sched = sb("sched", [P, 3 * NE + 2], I32)
        squares = sb("squares", [P, 768])
        pick_g = squares[:, :].rearrange("p (s i t) -> p s i t", s=2, i=NT)

        qT = scratch[:, 0:3072].rearrange("p (h t) -> p h t", h=8)
        kT = scratch[:, 3072:5632].rearrange("p (h t) -> p h t", h=5)
        prob = scratch[:, 5632:7168].rearrange("p (s c k) -> p s c k", s=2, c=2)
        proj_w_hi = d_ring_parts
        proj_in_hi = scratch_parts[:, 5632:8704].rearrange("p (k t) -> p k t", k=KD)
        pT = scratch[:, 7168:8704].rearrange("p (s c k) -> p s c k", s=2, c=2)
        y_sb = scratch[:, 0:3072].rearrange("p (b n f) -> p b n f", b=MAX_PAIRS, n=2)
        pick_gT = scratch[:, 3072:5376].rearrange("p (b n i t) -> p b n i t", b=MAX_PAIRS, n=2, i=NT)
        pick = scratch[:, 5376:6528].rearrange("p (i t) -> p i t", i=NT)
        sil = scratch[:, 6528:7040].rearrange("p (s f) -> p s f", s=2)
        hid = scratch[:, 7040:7552].rearrange("p (s f) -> p s f", s=2)
        hidT = scratch[:, 7552:8064].rearrange("p (s f t) -> p s f t", s=2, f=2)
        hidT_hi = scratch_parts[:, 7552:8064].rearrange("p (s f t) -> p s f t", s=2, f=2)
        hidT_lo = scratch_parts[:, 8064:8576].rearrange("p (s f t) -> p s f t", s=2, f=2)
        o_flat = o[:, :, :].rearrange("p i d -> p (i d)")
        ffn_in_hi = o_parts[:, :, :].rearrange("p i d -> p (i d)").rearrange("p (k t) -> p k t", k=KD)
        ln_par = o_flat[:, 0:2 * D].rearrange("p (a d) -> p a d", a=2)
        mixed = o_flat[:, 2 * D:3 * D]
        xg_rows = o_flat[:, 2 * D:3 * D].rearrange("p (s n) -> p s n", s=2)
        rope_a = o_flat[:, 0:512]
        rope_b = o_flat[:, 512:1024]
        qkv_flat = qkv[:, :, :].rearrange("p i d -> p (i d)")
        ffn_w_hi = [qkv_parts[:, :, :].rearrange("p i d -> p (i d)")[:, 0:6144], scratch_parts[:, 0:6144]]
        y_acc = qkv_flat[:, 0:NT * D].rearrange("p (i d) -> p i d", i=NT)
        h_tok = qkv_flat[:, NT * D:2 * NT * D].rearrange("p (i d) -> p i d", i=NT)

        ps = ctx.enter_context(nc.psum_tensor("ps", [P, 8, 512], F32))
        ident = cst[:, C_ID:C_ID + P]

        first_loaded = sem("first_loaded")
        params_loaded = sem("params_loaded")
        ln_loaded = sem("ln_loaded")
        gu_landed = [sem(f"gu_landed{k}") for k in range(GU_SLOTS)]
        d_landed = [sem(f"d_landed{k}") for k in range(D_SLOTS)]
        stored = sem("stored")
        dve_step = sem("dve_step")
        silu_done = sem("silu_done")
        ada_mm = sem("ada_mm")
        ada_row_copied = sem("ada_row_copied")
        ada_expanded = sem("ada_expanded")
        ada_exp_copied = sem("ada_exp_copied")
        x_ready = sem("x_ready")
        xT_mm = sem("xT_mm")
        hT_act = sem("hT_act")
        hT_dve = sem("hT_dve")
        qkv_mm = sem("qkv_mm")
        qkv_copied = sem("qkv_copied")
        post_done = sem("post_done")
        var_ready = sem("var_ready")
        rstd_ready = sem("rstd_ready")
        lam_sums = sem("lam_sums")
        lam_exps = sem("lam_exps")
        qt_mm = sem("qt_mm")
        qt_copied = sem("qt_copied")
        s_mm = sem("s_mm")
        max_done = sem("max_done")
        exp_done = sem("exp_done")
        soft_done = sem("soft_done")
        pT_mm = sem("pT_mm")
        pT_act = sem("pT_act")
        pT_dve = sem("pT_dve")
        o_mm = sem("o_mm")
        o_copied = sem("o_copied")
        oT_mm = sem("oT_mm")
        out_mm = sem("out_mm")
        gu_mm = sem("gu_mm")
        sil_ready = sem("sil_ready")
        hid_ready = sem("hid_ready")
        hidT_mm = sem("hidT_mm")
        hidT_copied = sem("hidT_copied")
        hidT_rest = sem("hidT_rest")
        weight_hi = sem("weight_hi")
        weight_lo = sem("weight_lo")
        input_hi = sem("input_hi")
        input_lo = sem("input_lo")
        proj_half_used = sem("proj_half_used")
        chunk_done = sem("chunk_done")
        router_loaded = sem("router_loaded")
        logit_mm = sem("logit_mm")
        top_ready = sem("top_ready")
        expo_ready = sem("expo_ready")
        chosen_ready = sem("chosen_ready")
        prefix_mm = sem("prefix_mm")
        sched_ready = sem("sched_ready")
        hTok_mm = sem("hTok_mm")
        hTok_copied = sem("hTok_copied")
        pick_ready = sem("pick_ready")
        pick_g_ready = sem("pick_g_ready")
        xg_rows_mm = sem("xg_rows_mm")
        xg_rows_copied = sem("xg_rows_copied")
        xgT_mm = sem("xgT_mm")
        xgT_copied = sem("xgT_copied")
        pgT_mm = sem("pgT_mm")
        pgT_copied = sem("pgT_copied")
        y_copied = sem("y_copied")
        spread_mm = sem("spread_mm")
        spread_added = sem("spread_added")

        gu_plan = []

        def ada_piece(l, j):
            src = w_ada[l].rearrange("(p k) n -> p k n", k=KD)[:, :, 512 * j:512 * j + 512]
            gu_plan.append((("w", src, 512), (ada_mm, 12 * l + j + 1)))

        DENSE = NT * NCH
        for l in range(DEPTH):
            for j in range(4):
                ada_piece(l, j)
            for n, (c0, w) in enumerate(PIECE_COLS):
                src = w_in[l].rearrange("(k p) n -> p k n", p=P)[:, :, c0:c0 + w]
                gu_plan.append((("w", src, w), (qkv_mm, 15 * l + 3 * n + 3)))
            for j in range(4, 12):
                ada_piece(l, j)
            for n in range(2):
                src = w_out[l].rearrange("(k p) n -> p k n", p=P)[:, :, 512 * n:512 * n + 512]
                gu_plan.append((("w", src, 512), (out_mm, 6 * l + 3 * n + 3)))
            if l == 0:
                for ch in range(NCH):
                    gu_plan.append((("f", ch, 0), (gu_mm, NT * ch + NT)))
        n_static = len(gu_plan)
        gu_slot = [(k - n_static + 2) % GU_SLOTS for k in range(n_static)]
        gu_value, used = [], [0] * GU_SLOTS
        for k in range(n_static):
            used[gu_slot[k]] += 1
            gu_value.append(32 * used[gu_slot[k]])
        gu_static = list(used)
        first_gu = {0: 0, 1: 19 + NCH}
        dense_gu = 19

        def piece_view(k, w=512):
            return gu_ring[:, gu_slot[k], 0:KD * w].rearrange("p (k n) -> p k n", k=KD)

        def chunk_view(slot):
            return gu_ring[:, slot, :].rearrange("p (k a f) -> p k a f", k=KD, a=2)

        def down_view(slot):
            return d_ring[:, slot, :].rearrange("p (f n) -> p f n", f=2)

        def gate_up_src(wg, wu, ch):
            return [w.rearrange("(k p) f -> p k f", p=P)[:, :, FC * ch:FC * ch + FC] for w in (wg, wu)]

        def down_src(wd, ch):
            return wd[FC * ch:FC * ch + FC, :].rearrange("(f p) n -> p f n", p=P)

        def proj_half(l, h):
            piece = h // 2 if h < 10 else 5 + (h - 10) // 2
            w = PIECE_COLS[piece][1] if piece < 5 else 512
            k = first_gu[l] + (4 + piece if piece < 5 else 17 + piece - 5)
            c0 = 4 * w * (h % 2)
            return (k, gu_ring[:, gu_slot[k], c0:c0 + 4 * w], gu_ring_parts[:, gu_slot[k], c0:c0 + 4 * w],
                    proj_w_hi[:, (PROJ_HALVES * l + h) % 3, 0:4 * w])

        def ffn_part(q):
            ch, part = divmod(q, 3)
            hi = ffn_w_hi[ch % 2][:, 2048 * part:2048 * part + 2048]
            if part == 2:
                return d_ring[:, ch % D_SLOTS, :], d_ring_parts[:, ch % D_SLOTS, :], hi
            k, c = gu_slot[dense_gu + ch], slice(2048 * part, 2048 * part + 2048)
            return gu_ring[:, k, c], gu_ring_parts[:, k, c], hi

        def each_block(eng, n_blocks, step):
            def rest(b):
                if b < MAX_BLOCKS:
                    with eng.If(n_blocks > b):
                        step(b)
                        rest(b + 1)
            step(0)
            rest(1)

        block = ctx.enter_context(nc.Block())

        @block.sync
        def _(sp):
            def load_chunk(slot, wg, wu, ch):
                for a, src in enumerate(gate_up_src(wg, wu, ch)):
                    sp.dma_start(chunk_view(slot)[:, :, a, :], src).then_inc(gu_landed[slot], 16)

            last_user = [None] * GU_SLOTS
            for k, ((kind, src, w), release) in enumerate(gu_plan):
                slot = gu_slot[k]
                if last_user[slot] is not None:
                    sp.wait_ge(*last_user[slot])
                last_user[slot] = release
                if kind == "w":
                    for a in range(2):
                        sp.dma_start(piece_view(k, w)[:, 4 * a:4 * a + 4, :],
                                     src[:, 4 * a:4 * a + 4, :]).then_inc(gu_landed[slot], 16)
                else:
                    load_chunk(slot, w_ffn_gate[0], w_ffn_up[0], src)
                    for ch in ([] if src == 0 else [src - 1] if src < NCH - 1 else [src - 1, src]):
                        if ch == 0:
                            sp.wait_ge(out_mm, 6)
                        if ch >= D_SLOTS:
                            sp.wait_ge(chunk_done, ch - D_SLOTS + 1)
                        sp.dma_start(down_view(ch % D_SLOTS), down_src(w_ffn_down[0], ch)).then_inc(
                            d_landed[ch % D_SLOTS], 16)
            sp.wait_ge(out_mm, 12)
            with sp.Fori(0, NE) as t:
                for ch in range(NCH):
                    before = ch - 3 if ch >= 3 else [9, 10, 8][ch] - NCH
                    sp.wait_ge(chunk_done, t * NCH + (NCH + before + 1))
                    load_chunk(ch % GU_SLOTS, w_moe_gate[0, t], w_moe_up[0, t], ch)
                    sp.dma_start(down_view(ch % D_SLOTS), down_src(w_moe_down[0, t], ch)).then_inc(
                        d_landed[ch % D_SLOTS], 16)

        @block.gpsimd
        def _(pool):
            n_rstd = [0]

            def rstds(n, width):
                for _ in range(n):
                    n_rstd[0] += 1
                    pool.wait_ge(var_ready, n_rstd[0])
                    pool.tensor_tensor(rstd[:, 0:width], var_in[:, 0:width], neg_half[:, 0:width],
                                       ALU.pow).then_inc(rstd_ready, 1)

            def load_params(l):
                src = [(lam_in[:, :, :], diff_lambda[l].rearrange("a d -> (a d)").partition_broadcast(P)
                        .rearrange("p (a d) -> p a d", a=4)),
                       (subln[:, :], diff_subln[l].partition_broadcast(P)),
                       (qk_gain[:, :, :], qk_norm_gain[l].rearrange("a d -> (a d)").partition_broadcast(P)
                        .rearrange("p (a d) -> p a d", a=2)),
                       (bada[:, :], b_ada[l].rearrange("(j n) -> j n", n=512)),
                       (cache_a[:, 0, :], cache_a_k[0, l].rearrange("t h c d -> t (h c d)")),
                       (cache_a[:, 1, :], cache_a_v[0, l].rearrange("t h d -> t (h d)")),
                       (cache_b[:, 0, :], cache_b_k[0, l].rearrange("t h d -> t (h d)")),
                       (cache_b[:, 1, :], cache_b_v[0, l].rearrange("t h d -> t (h d)"))]
                for dst, s in src:
                    pool.dma_start(dst, s).then_inc(params_loaded, 16)

            def load_ln(l, which):
                pool.dma_start(ln_par[:, 0, :], ln_gain[l, which].partition_broadcast(P)).then_inc(ln_loaded, 16)
                pool.dma_start(ln_par[:, 1, :], ln_bias[l, which].partition_broadcast(P)).then_inc(ln_loaded, 16)

            pool.dma_start(cst[:, :], consts).then_inc(first_loaded, 16)
            pool.dma_start(cond_raw[:, 0, :], c_ctx.rearrange("(p k) -> p k", k=KD)).then_inc(first_loaded, 16)
            pool.dma_start(cond_raw[:, 1, :], c[0].rearrange("(p k) -> p k", k=KD)).then_inc(first_loaded, 16)
            pool.dma_start(x[:, 0, :], x_prompt[0]).then_inc(first_loaded, 16)
            pool.dma_start(x[:, 1:3, :], x_sample[0].rearrange("(i p) d -> p i d", p=P)).then_inc(first_loaded, 16)
            pool.dma_start(w_rt[:, :, :], w_router[0].rearrange("(k p) e -> p k e", p=P)).then_inc(router_loaded, 16)
            for l in range(DEPTH):
                if l == 0:
                    load_params(0)
                rstds(3, 8)
                rstds(3, 2)
                pool.wait_ge(post_done, 10 * l + 10)
                pool.wait_ge(qkv_copied, 15 * l + 15)
                pool.dma_start(new_a_k[0, l].rearrange("t h c d -> t (h c d)"), qkv[:, 0, AK:AV]).then_inc(stored, 16)
                pool.dma_start(new_a_v[0, l].rearrange("t h d -> t (h d)"), qkv[:, 0, AV:BQ]).then_inc(stored, 16)
                pool.dma_start(new_b_k[0, l].rearrange("t h d -> t (h d)"), qkv[:, 0, BK:BV]).then_inc(stored, 16)
                pool.dma_start(new_b_v[0, l].rearrange("t h d -> t (h d)"), qkv[:, 0, BV:COLS]).then_inc(stored, 16)
                rstds(3, 4)
                pool.wait_ge(oT_mm, 6 * l + 6)
                load_ln(l, 0)
                rstds(3, 1)
                pool.wait_ge(x_ready, 6 * l + 3)
                if l == 0:
                    pool.wait_ge(ada_mm, 12)
                    load_params(1)
                    pool.wait_ge(gu_mm, DENSE)
                load_ln(l, 1)
                rstds(3, 1)
            pool.wait_ge(x_ready, 12)
            pool.dma_start(y_prompt[0], x[:, 0, :]).then_inc(stored, 16)
            pool.dma_start(y_sample[0].rearrange("(i p) d -> p i d", p=P), x[:, 1:3, :]).then_inc(stored, 16)
            pool.wait_ge(stored, 16 * (4 * DEPTH + 2))

        @block.scalar
        def _(act):
            def copy_ada_row(l, j):
                a = 12 * l + j
                act.wait_ge(ada_mm, a + 1)
                if j >= 10:
                    dst = gate2_rows[:, j - 10, :]
                    if l:
                        act.wait_ge(ada_expanded, 16)
                else:
                    dst = ada_row[:, :]
                    if a:
                        act.wait_ge(ada_expanded, 16 * l + ada_expands_before(j))
                act.activation(dst, ps[0:2, 7, :], ACT.Copy).then_inc(ada_row_copied, 1)

            def split_proj_weight(l, h):
                g = PROJ_HALVES * l + h
                k, value, _, hi = proj_half(l, h)
                act.wait_ge(gu_landed[gu_slot[k]], gu_value[k])
                if g >= 3:
                    lb, hb = divmod(g - 3, PROJ_HALVES)
                    if hb % 2 == 0:
                        act.wait_ge(proj_half_used, PROJ_HALVES // 2 * lb + hb // 2 + 1)
                    elif hb < 10:
                        act.wait_ge(qkv_mm, 15 * lb + 3 * (hb // 2) + 3)
                    else:
                        act.wait_ge(out_mm, 6 * lb + 3 * ((hb - 10) // 2) + 3)
                act.activation(hi, value, ACT.Copy).then_inc(weight_hi, 1)

            def split_ffn_weight(q):
                ch, part = divmod(q, 3)
                value, _, hi = ffn_part(q)
                if part < 2:
                    k = dense_gu + ch
                    act.wait_ge(gu_landed[gu_slot[k]], gu_value[k])
                    if ch >= 2:
                        act.wait_ge(gu_mm, NT * (ch - 1))
                else:
                    act.wait_ge(d_landed[ch % D_SLOTS], 16 * (ch // D_SLOTS + 1))
                    if ch >= 2:
                        act.wait_ge(chunk_done, ch - 1)
                act.activation(hi, value, ACT.Copy).then_inc(weight_hi, 1)

            def modulate(l, which):
                h = 2 * l + which
                hi = None if l and which else ffn_in_hi if which else proj_in_hi
                for kc in range(KD):
                    if kc % 2:
                        if hi is not None:
                            act.wait_ge(hT_dve, 4 * h + kc // 2 + 1)
                            act.activation(hi[:, kc, :], hT[:, kc, :], ACT.Copy).then_inc(input_hi, 1)
                        continue
                    act.wait_ge(xT_mm, 8 * h + kc + 1)
                    act.wait_ge(ada_exp_copied, 16 * l + (16 if which else 4))
                    b = 4 + kc % 2
                    act.activation(hT[:, kc, 0:P], ps[:, b, 0:P], ACT.Identity,
                                   bias=mod[:, 2 * which, kc, 0:1], scale=mod[:, 2 * which + 1, kc, 0:1])
                    act.activation(hT[:, kc, P:TOKENS], ps[:, b, P:TOKENS], ACT.Identity,
                                   bias=mod[:, 2 * which, kc, 1:2],
                                   scale=mod[:, 2 * which + 1, kc, 1:2]).then_inc(hT_act, 1)
                    if hi is not None:
                        act.wait_ge(hT_act, 4 * h + kc // 2 + 1)
                        act.activation(hi[:, kc, :], hT[:, kc, :], ACT.Copy).then_inc(input_hi, 1)

            def copy_qkv(l, n):
                c0, w = PIECE_COLS[n]
                for i in range(NT):
                    q = 15 * l + 3 * n + i
                    act.wait_ge(qkv_mm, q + 1)
                    dst, src = qkv[:, i, c0:c0 + w], ps[:, (3 * n + i) % 4, 0:w]
                    if n == 3:
                        dst = dst.rearrange("p (h g d) -> p g h d", g=GKV, d=HD)
                        src = src.rearrange("p (g h d) -> p g h d", g=GKV, d=HD)
                    act.activation(dst, src, ACT.Copy).then_inc(qkv_copied, 1)

            def copy_qt(l, gs):
                for g in gs:
                    n, i = GROUPS[g]
                    act.wait_ge(qt_mm, NGROUPS * l + g + 1)
                    t0 = P * i
                    dst = {0: qT[:, 0:4, t0:t0 + P], 1: kT[:, 0:4, t0:t0 + P], 3: qT[:, 4:8, t0:t0 + P],
                           4: kT[:, 4:5, t0:t0 + P], "ca": kT[:, 0:4, TOKENS:TOKENS + P],
                           "cb": kT[:, 4:5, TOKENS:TOKENS + P]}[n]
                    m = dst.shape[1]
                    act.activation(dst, ps[:, 4 + g % 4, 0:P * m].rearrange("p (h t) -> p h t", h=m),
                                   ACT.Copy).then_inc(qt_copied, 1)

            def exps(l, v):
                u = UNITS * l + v
                i, _ = tile_of_unit(v)
                nk = P if i == 0 else 3 * P
                act.wait_ge(max_done, u + 1)
                if v >= 2:
                    act.wait_ge(pT_mm, u - 1)
                for cc in range(2):
                    ins = act.activation(prob[:, v % 2, cc, 0:nk], ps[:, 2 * (v % 2) + cc, 0:nk], ACT.Exp,
                                         bias=nbias[:, v % 2, cc:cc + 1], scale=SCALE,
                                         accum_out=rsum[:, v % 4, cc:cc + 1])
                ins.then_inc(exp_done, 1)

            def copy_pT(l, v):
                u = UNITS * l + v
                i, pr = tile_of_unit(v)
                nk = P if i == 0 else 3 * P
                act.wait_ge(pT_mm, u + 1)
                if v >= 2:
                    act.wait_ge(o_mm, u - 1)
                cc = 1 if pr >= 4 else 0
                act.activation(pT[:, v % 2, cc, 0:nk], ps[:, 4 + cc, 0:nk], ACT.Copy).then_inc(pT_act, 1)

            def copy_hiddenT(s, k, w):
                act.wait_ge(hidT_mm, s + 1)
                dst = (hidT_hi if w == FC else hidT)[:, k % 2, :, :].rearrange("p f t -> p (f t)")[:, 0:w]
                act.activation(dst, ps[:, 6 + k % 2, 0:w], ACT.Copy).then_inc(hidT_copied, 1)

            def silu(s, k, w):
                act.wait_ge(gu_mm, s + 1)
                act.activation(sil[:, k % 2, 0:w], ps[:, 6 + k % 2, 0:w], ACT.Silu).then_inc(sil_ready, 1)

            act.wait_ge(first_loaded, 80)
            act.activation(cond[:, :, :], cond_raw[:, :, :].rearrange("p a k -> p k a"), ACT.Silu).then_inc(silu_done, 1)
            for l in range(DEPTH):
                for j in range(4):
                    copy_ada_row(l, j)
                split_proj_weight(l, 0)
                split_proj_weight(l, 1)
                modulate(l, 0)
                split_proj_weight(l, 2)
                act.wait_ge(params_loaded, 128 * (l + 1))
                act.wait_ge(lam_sums, l + 1)
                act.activation(lam_exp[:, :], lam_sum[:, :], ACT.Exp).then_inc(lam_exps, 1)
                if l:
                    act.wait_ge(stored, 64)
                for n, gs in enumerate(QT_AFTER):
                    if 2 * n + 3 < 10:
                        split_proj_weight(l, 2 * n + 3)
                    copy_qkv(l, n)
                    if 2 * n + 4 < 10:
                        split_proj_weight(l, 2 * n + 4)
                    copy_qt(l, gs)
                for v in range(UNITS + 1):
                    if v < UNITS:
                        exps(l, v)
                    if v % 3 == 1:
                        copy_ada_row(l, 4 + v // 3)
                    if v >= 1:
                        copy_pT(l, v - 1)
                    if v >= UNITS - 1:
                        split_proj_weight(l, 10 + v - (UNITS - 1))
                for i in range(NT):
                    for hf in range(2):
                        act.wait_ge(oT_mm, 6 * l + 2 * i + hf + 1)
                        act.activation(proj_in_hi[:, 4 * hf:4 * hf + 4, P * i:P * i + P],
                                       ps[:, 2 * i + hf, :].rearrange("p (k t) -> p k t", k=4),
                                       ACT.Copy).then_inc(input_hi, 1)
                split_proj_weight(l, 12)
                split_proj_weight(l, 13)
                if l == 0:
                    act.wait_ge(stored, 64)
                    split_ffn_weight(0)
                    split_ffn_weight(1)
                modulate(l, 1)
                if l == 0:
                    split_ffn_weight(2)
                    for s in range(DENSE + 1):
                        if s:
                            copy_hiddenT(s - 1, s - 1, FC)
                        if s + 3 < DENSE:
                            split_ffn_weight(s + 3)
                        if s < DENSE:
                            silu(s, s, FC)
            for k in range(6):
                act.wait_ge(hTok_mm, k + 1)
                act.activation(h_tok[:, k // 2, 512 * (k % 2):512 * (k % 2) + 512], ps[:, 1 + k, :],
                               ACT.Copy).then_inc(hTok_copied, 1)
            act.wait_ge(top_ready, 1)
            act.activation(expo[:, :, :], expo[:, :, :], ACT.Exp).then_inc(expo_ready, 1)
            act.wait_ge(sched_ready, 1)

            def gathered(nb, b0):
                def rows(b):
                    act.wait_ge(xg_rows_mm, b0 + (b + 1))
                    act.activation(xg_rows[:, b % 2, :], ps[:, 6 + b % 2, :], ACT.Copy).then_inc(xg_rows_copied, 1)

                def turned(b):
                    act.wait_ge(xgT_mm, b0 + (b + 1))
                    act.activation(hT[:, :, BT * b:BT * b + BT].rearrange("p (n m) t -> p m n t", n=2),
                                   ps[:, 6 + b % 2, :].rearrange("p (m n t) -> p m n t", m=4, n=2),
                                   ACT.Copy).then_inc(xgT_copied, 1)

                def rest(b):
                    if b + 1 < MAX_BLOCKS:
                        with act.If(nb > b + 1):
                            rows(b + 1)
                            turned(b)
                            rest(b + 1)
                        with act.Else():
                            turned(b)
                    else:
                        turned(b)

                rows(0)
                rest(0)

            nb0 = act.value_load(sched[0:1, 0:1], min_val=1, max_val=MAX_BLOCKS)
            gathered(nb0, 0)
            with act.Fori(0, NE) as t:
                nb = act.value_load(sched[0:1, bass.ds(t, 1)], min_val=1, max_val=MAX_BLOCKS)
                b0 = act.value_load(sched[0:1, bass.ds(t + (NE + 1), 1)], min_val=0, max_val=MAX_BLOCKS * NE)
                for ch in range(NCH):
                    s0 = b0 * NCH + nb * ch + DENSE

                    def rest(b):
                        copy_hiddenT(s0 + b, b, P)
                        if b + 1 < MAX_BLOCKS:
                            with act.If(nb > b + 1):
                                silu(s0 + (b + 1), b + 1, P)
                                rest(b + 1)

                    silu(s0, 0, P)
                    rest(0)
                act.wait_ge(chunk_done, t * NCH + 2 * NCH)

                def copy_y(b):
                    for h in range(2):
                        lo = BT * h
                        ins = act.activation(y_sb[lo:lo + BT, b // 2, (h + b) % 2, :], ps[lo:lo + BT, b, :], ACT.Copy)
                    ins.then_inc(y_copied, 1)

                each_block(act, nb, copy_y)
                nb_next = act.value_load(sched[0:1, bass.ds(t + 1, 1)], min_val=1, max_val=MAX_BLOCKS)
                gathered(nb_next, b0 + nb)

        @block.vector
        def _(dve):
            chain = [0]
            n_rstd = [0]

            def link(ins):
                chain[0] += 1
                ins.then_inc(dve_step, 1)
                dve.wait_ge(dve_step, chain[0])

            def rstd_of(width, mean_scale, src):
                dve.tensor_scalar(var_in[:, 0:width], src, mean_scale, EPS, ALU.mult, ALU.add).then_inc(var_ready, 1)
                n_rstd[0] += 1
                dve.wait_ge(rstd_ready, n_rstd[0])

            def copy_expansion(l, k):
                dve.wait_ge(ada_expanded, 16 * l + k + 1)
                if k < 4 or 8 <= k < 12:
                    j = k if k < 4 else k - 2
                    s = j // 2 if j < 4 else j // 2 - 1
                    dst = mod[:, s, 4 * (j % 2):4 * (j % 2) + 4, :]
                    ins = dve.tensor_scalar(dst, ps[:, 7, 0:8].rearrange("p (k a) -> p k a", a=2),
                                            float(s % 2), None, ALU.add)
                else:
                    k4 = k % 4
                    ins = dve.tensor_copy(gate[:, k4 % 2, 512 * (k4 // 2):512 * (k4 // 2) + 512], ps[:, 7, :])
                ins.then_inc(ada_exp_copied, 1)

            n_weight, n_input = [0], [0]

            def weight_rest(value, lo, hi):
                n_weight[0] += 1
                dve.wait_ge(weight_hi, n_weight[0])
                dve.tensor_tensor(lo, value, hi.bitcast(F32), ALU.subtract).then_inc(weight_lo, 1)

            def input_rest(dst, value, hi):
                n_input[0] += 1
                dve.wait_ge(input_hi, n_input[0])
                dve.tensor_tensor(dst, value, hi.bitcast(F32), ALU.subtract).then_inc(input_lo, 1)

            def modulate(l, which):
                h = 2 * l + which
                hi = None if l and which else ffn_in_hi if which else proj_in_hi
                dve.wait_ge(ada_exp_copied, 16 * l + (16 if which else 4))
                for kc in range(1, KD, 2):
                    dve.wait_ge(xT_mm, 8 * h + kc + 1)
                    b = 4 + kc % 2
                    dve.tensor_scalar(hT[:, kc, 0:P], ps[:, b, 0:P], mod[:, 2 * which + 1, kc, 0:1],
                                      mod[:, 2 * which, kc, 0:1], ALU.mult, ALU.add)
                    dve.tensor_scalar(hT[:, kc, P:TOKENS], ps[:, b, P:TOKENS], mod[:, 2 * which + 1, kc, 1:2],
                                      mod[:, 2 * which, kc, 1:2], ALU.mult, ALU.add).then_inc(hT_dve, 1)
                    if hi is not None:
                        for q in ([0] if kc == 1 else [kc - 2, kc - 1]):
                            input_rest(hT_parts[:, q, :], hT[:, q, :], hi[:, q, :])
                if hi is not None:
                    input_rest(hT_parts[:, KD - 1, :], hT[:, KD - 1, :], hi[:, KD - 1, :])

            def rope(i, c0, heads):
                w = heads * HD
                v = qkv[:, i, c0:c0 + w].rearrange("p (h d) -> p h d", d=HD)
                v4 = qkv[:, i, c0:c0 + w].rearrange("p (h a s d) -> p h a s d", a=2, s=2, d=16)
                ta = rope_a[:, 0:w].rearrange("p (h d) -> p h d", d=HD)
                tb = rope_b[:, 0:w].rearrange("p (h a s d) -> p h a s d", a=2, s=2, d=16)
                cos = cst[:, C_COS + HD * (i - 1):C_COS + HD * i].unsqueeze(1).broadcast_to([P, heads, HD])
                sin = cst[:, C_SIN + HD * (i - 1):C_SIN + HD * i].rearrange("p (a s d) -> p a s d", a=2, s=2)
                dve.tensor_tensor(ta, v, cos, ALU.mult)
                for s in range(2):
                    ins = dve.tensor_tensor(
                        tb[:, :, :, s, :], v4[:, :, :, 1 - s, :],
                        sin[:, :, s, :].unsqueeze(1).broadcast_to([P, heads, 2, 16]), ALU.mult)
                link(ins)
                return dve.tensor_tensor(v, ta, rope_b[:, 0:w].rearrange("p (h d) -> p h d", d=HD), ALU.add)

            def head_norm(v, heads, width, gain, extra):
                sq = rope_a[:, 0:heads * width].rearrange("p (h d) -> p h d", d=width)
                link(dve.tensor_tensor(sq, v, v, ALU.mult))
                link(dve.tensor_reduce(var_in[:, 0:heads], sq, AX, ALU.add))
                rstd_of(heads, 1.0 / width, var_in[:, 0:heads])
                link(dve.tensor_tensor(v, v, rstd[:, 0:heads].unsqueeze(2).broadcast_to([P, heads, width]), ALU.mult))
                return dve.scalar_tensor_tensor(out=v, in0=v, scalar=extra,
                                                in1=gain.unsqueeze(1).broadcast_to([P, heads, width]),
                                                op0=ALU.mult, op1=ALU.mult)

            def post(l, n, i):
                dve.wait_ge(qkv_copied, 15 * l + 3 * n + i + 1)
                c0 = {0: AQ, 1: AK, 3: BQ, 4: BK}[n]
                heads = {0: 8, 1: 8, 3: GH, 4: GKV}[n]
                ins = None
                if n >= 3:
                    v = qkv[:, i, c0:c0 + heads * HD].rearrange("p (h d) -> p h d", d=HD)
                    ins = head_norm(v, heads, HD, qk_gain[:, n - 3, :], 1.0)
                    if i:
                        link(ins)
                if i:
                    ins = rope(i, c0, heads)
                ins.then_inc(post_done, 1)
                dve.wait_ge(post_done, 10 * l + POSTS.index((n, i)) + 1)

            def lam(l):
                dve.wait_ge(params_loaded, 128 * (l + 1))
                for a in range(2):
                    ins = dve.tensor_tensor(lam_tmp[:, a, :], lam_in[:, 2 * a, :], lam_in[:, 2 * a + 1, :], ALU.mult)
                link(ins)
                dve.tensor_reduce(lam_sum[:, :], lam_tmp[:, :, :], AX, ALU.add).then_inc(lam_sums, 1)
                dve.wait_ge(lam_exps, l + 1)
                lam_init = 0.8 - 0.6 * math.exp(-0.3 * l)
                link(dve.tensor_tensor(neg_lam[:, :], lam_exp[:, 1:2], lam_exp[:, 0:1], ALU.subtract))
                link(dve.tensor_scalar(neg_lam[:, :], neg_lam[:, :], -lam_init, None, ALU.add))

            def row_max(l, v):
                u = UNITS * l + v
                i, _ = tile_of_unit(v)
                nk = P if i == 0 else 3 * P
                dve.wait_ge(s_mm, u + 1)
                b = 2 * (v % 2)
                link(dve.tensor_reduce(smax[:, v % 2, :], ps[:, b:b + 2, 0:nk], AX, ALU.max))
                dve.tensor_scalar(nbias[:, v % 2, :], smax[:, v % 2, :], -SCALE, None, ALU.mult).then_inc(max_done, 1)

            def combine(l, v):
                u = UNITS * l + v
                i, pr = tile_of_unit(v)
                nk = P if i == 0 else 3 * P
                dve.wait_ge(exp_done, u + 1)
                ins = dve.reciprocal(rinv[:, v % 4, :], rsum[:, v % 4, :])
                if pr < 4:
                    link(ins)
                    link(dve.tensor_tensor(rlam[:, :], rinv[:, v % 4, 1:2], neg_lam[:, :], ALU.mult))
                    p1, p0 = prob[:, v % 2, 1, 0:nk], prob[:, v % 2, 0, 0:nk]
                    link(dve.tensor_scalar(p1, p1, rlam[:, 0:1], None, ALU.mult))
                    ins = dve.scalar_tensor_tensor(out=p0, in0=p0, scalar=rinv[:, v % 4, 0:1], in1=p1,
                                                   op0=ALU.mult, op1=ALU.add)
                ins.then_inc(soft_done, 1)

            def copy_pT(l, v):
                u = UNITS * l + v
                i, pr = tile_of_unit(v)
                nk = P if i == 0 else 3 * P
                if pr >= 4:
                    dve.wait_ge(pT_mm, u + 1)
                    dve.tensor_copy(pT[:, v % 2, 0, 0:nk], ps[:, 4, 0:nk]).then_inc(pT_dve, 1)

            def copy_o(l, v):
                u = UNITS * l + v
                i, pr = tile_of_unit(v)
                dve.wait_ge(o_mm, u + 1)
                if pr < 4:
                    dve.tensor_copy(o[:, i, P * pr:P * pr + P], ps[:, 6, 0:P]).then_inc(o_copied, 1)
                    if pr == 3:
                        dve.wait_ge(o_copied, u + 1)
                        lam_init = 0.8 - 0.6 * math.exp(-0.3 * l)
                        v3 = o[:, i, 0:DW].rearrange("p (h d) -> p h d", d=2 * HD)
                        sq = squares[:, 0:DW].rearrange("p (h d) -> p h d", d=2 * HD)
                        link(dve.tensor_tensor(sq, v3, v3, ALU.mult))
                        link(dve.tensor_reduce(var_in[:, 0:DH], sq, AX, ALU.add))
                        rstd_of(DH, 1.0 / (2 * HD), var_in[:, 0:DH])
                        link(dve.tensor_tensor(v3, v3, rstd[:, 0:DH].unsqueeze(2).broadcast_to([P, DH, 2 * HD]),
                                               ALU.mult))
                        link(dve.scalar_tensor_tensor(out=v3, in0=v3, scalar=1.0 - lam_init,
                                                      in1=subln[:, :].unsqueeze(1).broadcast_to([P, DH, 2 * HD]),
                                                      op0=ALU.mult, op1=ALU.mult))
                else:
                    for cc in range(2):
                        hq = pr - 4 + 4 * cc
                        ins = dve.tensor_scalar(o[:, i, DW + HD * hq:DW + HD * hq + HD],
                                                ps[:, 6, HD * cc:HD * cc + HD],
                                                rinv[:, v % 4, cc:cc + 1], None, ALU.mult)
                    ins.then_inc(o_copied, 1)

            def residual(l, which, source, waits, between=lambda i: None):
                e = 2 * l + which
                dve.wait_ge(ln_loaded, 32 * (e + 1))
                for i in range(NT):
                    waits(i)
                    cd = 0 if i == 0 else 1
                    link(dve.tensor_tensor(mixed.rearrange("p (a n) -> p a n", a=2), source(i),
                                           gate[:, cd, :].rearrange("p (a n) -> p a n", a=2), ALU.mult))
                    link(dve.scalar_tensor_tensor(out=x[:, i, :], in0=x[:, i, :], scalar=ALPHA, in1=mixed,
                                                  op0=ALU.mult, op1=ALU.add))
                    for a in range(2):
                        ins = dve.bn_stats(stats[:, a, :], x[:, i, 512 * a:512 * a + 512])
                    link(ins)
                    link(dve.bn_aggr(mv[:, :], stats[:, :, :]))
                    rstd_of(1, 1.0, mv[:, 1:2])
                    link(dve.tensor_scalar(x[:, i, :], x[:, i, :], mv[:, 0:1], rstd[:, 0:1],
                                           ALU.subtract, ALU.mult))
                    link(dve.tensor_tensor(x[:, i, :], x[:, i, :], ln_par[:, 0, :], ALU.mult))
                    dve.tensor_tensor(x[:, i, :], x[:, i, :], ln_par[:, 1, :], ALU.add).then_inc(x_ready, 1)
                    dve.wait_ge(x_ready, 3 * e + i + 1)
                    between(i)

            def ffn_mul(s, k, w):
                dve.wait_ge(sil_ready, s + 1)
                dve.tensor_tensor(hid[:, k % 2, 0:w], sil[:, k % 2, 0:w], ps[:, 6 + k % 2, w:2 * w],
                                  ALU.mult).then_inc(hid_ready, 1)

            link(dve.memset(neg_half[:, :], -0.5))
            link(dve.memset(var_in[:, :], 1.0))
            dve.wait_ge(first_loaded, 80)
            for l in range(DEPTH):
                if l == 0:
                    for k in range(4):
                        copy_expansion(l, k)
                weight_rest(*proj_half(l, 0)[1:])
                weight_rest(*proj_half(l, 1)[1:])
                modulate(l, 0)
                weight_rest(*proj_half(l, 2)[1:])
                lam(l)
                for n in range(5):
                    if 2 * n + 3 < 10:
                        weight_rest(*proj_half(l, 2 * n + 3)[1:])
                    for m, i in POSTS:
                        if m == n:
                            post(l, n, i)
                    if 2 * n + 4 < 10:
                        weight_rest(*proj_half(l, 2 * n + 4)[1:])
                for v in range(UNITS + 3):
                    if v < UNITS:
                        row_max(l, v)
                    if 2 <= v < UNITS + 2:
                        copy_pT(l, v - 2)
                    if 1 <= v <= UNITS:
                        combine(l, v - 1)
                    if v >= 3:
                        copy_o(l, v - 3)
                    q, r = divmod(v, 3)
                    if q < 8 and r == 2:
                        for k in EXPAND_OF[4 + q]:
                            copy_expansion(l, k)
                weight_rest(*proj_half(l, 10)[1:])
                weight_rest(*proj_half(l, 11)[1:])
                for i in range(NT):
                    for hf in range(2):
                        part = (slice(None), slice(4 * hf, 4 * hf + 4), slice(P * i, P * i + P))
                        input_rest(hT_parts[part], ps[:, 2 * i + hf, :].rearrange("p (k t) -> p k t", k=4),
                                   proj_in_hi[part])
                weight_rest(*proj_half(l, 12)[1:])
                weight_rest(*proj_half(l, 13)[1:])
                if l == 0:
                    weight_rest(*ffn_part(0))
                    weight_rest(*ffn_part(1))
                residual(l, 0, lambda i: ps[:, 2 * i:2 * i + 2, :],
                         lambda i: dve.wait_ge(out_mm, 6 * l + 3 + i + 1))
                for k in range(12, 16):
                    copy_expansion(l, k)
                modulate(l, 1)
                if l == 0:
                    weight_rest(*ffn_part(2))
                    for s in range(DENSE + 1):
                        if s:
                            dve.wait_ge(hidT_copied, s)
                            b = (s - 1) % 2
                            dve.tensor_tensor(hidT_lo[:, b, :, :],
                                              ps[:, 6 + b, 0:FC].rearrange("p (f t) -> p f t", f=2),
                                              hidT_hi[:, b, :, :].bitcast(F32), ALU.subtract).then_inc(hidT_rest, 1)
                        if s + 3 < DENSE:
                            weight_rest(*ffn_part(s + 3))
                        if s < DENSE:
                            ffn_mul(s, s, FC)

                    def next_expansions(i):
                        for k in ([0], [1], [2, 3])[i]:
                            copy_expansion(1, k)

                    residual(l, 1, lambda i: ps[:, 2 * i:2 * i + 2, :],
                             lambda i: dve.wait_ge(chunk_done, NCH), next_expansions)

            dve.wait_ge(logit_mm, 1)
            link(dve.tensor_copy(logit[:, :, :], ps[:, 0, 0:NT * NE].rearrange("p (i e) -> p i e", i=NT)))
            link(dve.tensor_reduce(top[:, :], logit[:, :, :], AX, ALU.max))
            dve.tensor_tensor(expo[:, :, :], logit[:, :, :], top[:, :].unsqueeze(2).broadcast_to([P, NT, NE]),
                              ALU.subtract).then_inc(top_ready, 1)
            pr3 = pair[:, :].rearrange("p (i e f) -> p i e f", i=NT, e=NE)
            pr4 = pair2[:, :].rearrange("p (i e f) -> p i e f", i=NT, e=NE)
            for i in range(NT):
                other = logit[:, i, :].unsqueeze(1).broadcast_to([P, NE, NE])
                own = logit[:, i, :].unsqueeze(2).broadcast_to([P, NE, NE])
                dve.tensor_tensor(pr3[:, i], other, own, ALU.is_gt)
                ins = dve.tensor_tensor(pr4[:, i], other, own, ALU.is_equal)
            link(ins)
            low = cst[:, C_LOW:C_LOW + 64]
            link(dve.tensor_tensor(pair2[:, :].rearrange("p (i q) -> p i q", i=NT),
                                   pair2[:, :].rearrange("p (i q) -> p i q", i=NT),
                                   low.unsqueeze(1).broadcast_to([P, NT, 64]), ALU.mult))
            link(dve.tensor_tensor(pair[:, :], pair[:, :], pair2[:, :], ALU.add))
            link(dve.tensor_reduce(place[:, :, :].rearrange("p i e -> p (i e)"),
                                   pair[:, :].rearrange("p (q f) -> p q f", f=NE), AX, ALU.add))
            dve.tensor_scalar(chosen[:, :, :], place[:, :, :], 1.5, None, ALU.is_lt).then_inc(chosen_ready, 1)
            dve.wait_ge(chosen_ready, 1)
            dve.wait_ge(expo_ready, 1)
            link(dve.tensor_tensor(gates[:, :, :], expo[:, :, :], chosen[:, :, :], ALU.mult))
            link(dve.tensor_reduce(gsum[:, :], gates[:, :, :], AX, ALU.add))
            link(dve.reciprocal(gsum[:, :], gsum[:, :]))
            link(dve.tensor_tensor(gates[:, :, :], gates[:, :, :], gsum[:, :].unsqueeze(2).broadcast_to([P, NT, NE]),
                                   ALU.mult))
            dve.wait_ge(prefix_mm, 1)
            ranks = rank[:, :, 0:NE]
            link(dve.memset(rank[:, :, :], 0.0))
            link(dve.tensor_scalar(ranks, ps[:, 0, 32:32 + NT * NE].rearrange("p (i e) -> p i e", i=NT),
                                   10000.0, None, ALU.add))
            link(dve.tensor_tensor(ranks, ranks, chosen[:, :, :], ALU.mult))
            link(dve.tensor_scalar(rank[:, :, :], rank[:, :, :], -10000.0, None, ALU.add))
            link(dve.tensor_copy(counts[:, :], ps[:, 0, 64:64 + NE]))
            link(dve.memset(blocks[:, NE:NE + 1], 1.0))
            nblk = blocks[:, 0:NE]
            link(dve.tensor_scalar(nblk, counts[:, :], BT + 0.5, 1.0, ALU.is_gt, ALU.add))
            for b in range(2, MAX_BLOCKS):
                link(dve.scalar_tensor_tensor(out=nblk, in0=counts[:, :], scalar=BT * b + 0.5,
                                              in1=nblk, op0=ALU.is_gt, op1=ALU.add))
            low3 = pair[:, 0:64].rearrange("p (e f) -> p e f", e=NE)
            link(dve.tensor_tensor(low3, nblk.unsqueeze(1).broadcast_to([P, NE, NE]),
                                   low.rearrange("p (e f) -> p e f", e=NE), ALU.mult))
            link(dve.tensor_reduce(cum[:, 0:NE], low3, AX, ALU.add))
            link(dve.tensor_reduce(cum[:, NE:NE + 1], nblk, AX, ALU.add))
            link(dve.tensor_scalar(pairs[:, :], counts[:, :], 2 * BT + 0.5, 1.0, ALU.is_gt, ALU.add))
            link(dve.scalar_tensor_tensor(out=pairs[:, :], in0=counts[:, :], scalar=4 * BT + 0.5,
                                          in1=pairs[:, :], op0=ALU.is_gt, op1=ALU.add))
            link(dve.tensor_tensor(low3, pairs[:, :].unsqueeze(1).broadcast_to([P, NE, NE]),
                                   low.rearrange("p (e f) -> p e f", e=NE), ALU.mult))
            link(dve.tensor_reduce(pair_cum[:, :], low3, AX, ALU.add))
            dve.memset(y_acc[:, :, :], 0.0).then_inc(spread_added, 1)
            dve.memset(y_sb[:, :, :, :], 0.0)
            dve.tensor_copy(sched[:, 2 * NE + 2:3 * NE + 2], pair_cum[:, :])
            link(dve.tensor_copy(sched[:, 0:NE + 1], blocks[:, :]))
            dve.tensor_copy(sched[:, NE + 1:2 * NE + 2], cum[:, :]).then_inc(sched_ready, 1)
            dve.wait_ge(sched_ready, 1)

            def select(e):
                for i in range(NT):
                    ins = dve.tensor_scalar(pick[:, i, :], cst[:, C_IOTA:C_IOTA + TOKENS], rank[:, i, e], None,
                                            ALU.is_equal)
                ins.then_inc(pick_ready, 1)

            select(slice(0, 1))
            with dve.Fori(0, NE) as t:
                nb = dve.value_load(sched[0:1, bass.ds(t, 1)], min_val=1, max_val=MAX_BLOCKS)
                b0 = dve.value_load(sched[0:1, bass.ds(t + (NE + 1), 1)], min_val=0, max_val=MAX_BLOCKS * NE)
                p0 = dve.value_load(sched[0:1, bass.ds(t + (2 * NE + 2), 1)], min_val=0, max_val=MAX_PAIRS * NE)

                def select_gates(b):
                    if b >= 2:
                        dve.wait_ge(pgT_mm, p0 + (b - 1))
                    for i in range(NT):
                        ins = dve.tensor_scalar(pick_g[:, b % 2, i, :], cst[:, C_IOTA + P * b:C_IOTA + P * b + P],
                                                rank[:, i, bass.ds(t, 1)], gates[:, i, bass.ds(t, 1)],
                                                ALU.is_equal, ALU.mult)
                    ins.then_inc(pick_g_ready, 1)

                def copy_gates(b):
                    dve.wait_ge(pgT_mm, p0 + (b + 1))
                    for n in range(2):
                        ins = dve.tensor_copy(pick_gT[:, b, n, :, :],
                                              ps[:, 6 + n, 0:NT * P].rearrange("p (i t) -> p i t", i=NT))
                    ins.then_inc(pgT_copied, 1)

                def copy_gates_from(b):
                    copy_gates(b)
                    if b + 1 < MAX_PAIRS:
                        with dve.If(nb > 2 * b + 2):
                            if b == 0:
                                with dve.If(nb > 4):
                                    select_gates(2)
                            copy_gates_from(b + 1)

                for ch in range(NCH):
                    s0 = b0 * NCH + nb * ch + DENSE
                    each_block(dve, nb, lambda b: ffn_mul(s0 + b, b, P))
                    if ch == 0:
                        select(bass.ds(t + 1, 1))
                        select_gates(0)
                        with dve.If(nb > 2):
                            select_gates(1)
                copy_gates_from(0)
                dve.wait_ge(spread_added, t * 6 + 1)
                for k in range(6):
                    dve.wait_ge(spread_mm, t * 6 + (k + 1))
                    ya = y_acc[:, k // 2, 512 * (k % 2):512 * (k % 2) + 512]
                    dve.tensor_tensor(ya, ya, ps[:, k, :], ALU.add).then_inc(spread_added, 1)
            dve.wait_ge(spread_added, 6 * NE + 1)
            residual(1, 1, lambda i: y_acc[:, i, :].rearrange("p (a n) -> p a n", a=2), lambda i: None)

        @block.tensor
        def _(pe):
            def ada_rows(l, j, k):
                a = 12 * l + j
                pe.wait_ge(gu_landed[gu_slot[k]], gu_value[k])
                if a:
                    pe.wait_ge(ada_row_copied, a)
                    pe.wait_ge(ada_exp_copied, 16 * l + ada_expands_before(j))
                w = piece_view(k)
                for kc in range(KD):
                    pe.matmul(ps[0:2, 7, :], cond[:, kc, :], w[:, kc, :], start=(kc == 0), stop=False)
                pe.matmul(ps[0:2, 7, :], cst[0:12, C_PIECE + 2 * j:C_PIECE + 2 * j + 2], bada[:, :],
                          start=False, stop=True).then_inc(ada_mm, 1)

            def ada_expand(l, k):
                if k < 4 or 8 <= k < 12:
                    j = k if k < 4 else k - 2
                    pe.wait_ge(ada_row_copied, 12 * l + j + 1)
                    for q in range(4):
                        ins = pe.transpose(ps[:, 7, 2 * q:2 * q + 2], ada_row[:, P * q:P * q + P],
                                           cst[0:2, C_ID:C_ID + 2])
                else:
                    half, cd = k % 4 // 2, k % 2
                    if k < 8:
                        pe.wait_ge(ada_row_copied, 12 * l + 4 + half + 1)
                        row = ada_row[:, :]
                    else:
                        pe.wait_ge(ada_row_copied, 12 * l + 12)
                        row = gate2_rows[:, half, :]
                    pe.wait_ge(ada_exp_copied, 16 * l + k)
                    ins = pe.matmul(ps[:, 7, :], cst[0:2, C_SEL + P * cd:C_SEL + P * cd + P], row,
                                    start=True, stop=True)
                ins.then_inc(ada_expanded, 1)

            def turn_x(l, which):
                h = 2 * l + which
                if h:
                    pe.wait_ge(x_ready, 3 * h)
                for kc in range(KD):
                    if kc >= 2:
                        pe.wait_ge(hT_dve if kc % 2 else hT_act, 4 * h + kc // 2)
                    for i in range(NT):
                        ins = pe.transpose(ps[:, 4 + kc % 2, P * i:P * i + P], x[:, i, P * kc:P * kc + P], ident)
                    ins.then_inc(xT_mm, 1)
                pe.wait_ge(hT_act, 4 * h + 4)
                pe.wait_ge(hT_dve, 4 * h + 4)

            def split_products(out, a_hi, a_lo, w_hi, w_lo, start, stop):
                terms = [(a_hi, w_hi), (a_hi, w_lo), (a_lo, w_hi)]
                for n, (a, w) in enumerate(terms):
                    ins = pe.matmul(out, a, w, start=(start and n == 0),
                                    stop=(stop and n == 2))
                return ins

            def project_half(l, h, banks, before, done):
                _, _, lo, hi = proj_half(l, h)
                w = lo.shape[1] // 4
                lo = lo.rearrange("p (k n) -> p k n", k=4)
                hi = hi.rearrange("p (k n) -> p k n", k=4)
                pe.wait_ge(weight_lo, WEIGHT_PARTS * l + h + 1)
                for i in range(NT):
                    before(i)
                    for q in range(4):
                        kc = 4 * (h % 2) + q
                        t = slice(P * i, P * i + P)
                        ins = split_products(ps[:, banks[i], 0:w], proj_in_hi[:, kc, t], hT_parts[:, kc, t], hi[:, q, :],
                                             lo[:, q, :], kc == 0, kc == KD - 1)
                    if h % 2:
                        ins.then_inc(done, 1)
                    elif i == NT - 1:
                        ins.then_inc(proj_half_used, 1)

            def project(l, n):
                def bank_free(i):
                    q = 3 * n + i
                    if q >= 4:
                        pe.wait_ge(qkv_copied, 15 * l + q - 3)

                for half in range(2):
                    project_half(l, 2 * n + half, [(3 * n + i) % 4 for i in range(NT)],
                                 bank_free if half == 0 else lambda i: None, qkv_mm)

            def turn_qk(l, gs):
                for g in gs:
                    n, i = GROUPS[g]
                    if (n, i) in POSTS:
                        pe.wait_ge(post_done, 10 * l + POSTS.index((n, i)) + 1)
                    elif n in (0, 1):
                        pe.wait_ge(qkv_copied, 15 * l + 3 * n + i + 1)
                    if g >= 4:
                        pe.wait_ge(qt_copied, NGROUPS * l + g - 3)
                    for m in range(1 if n in (4, "cb") else 4):
                        src = {0: qkv[:, i, AQ + P * m:AQ + P * m + P], 1: qkv[:, i, AK + P * m:AK + P * m + P],
                               3: qkv[:, i, BQ + P * m:BQ + P * m + P],
                               4: qkv[:, i, BK:BK + P], "ca": cache_a[:, 0, P * m:P * m + P],
                               "cb": cache_b[:, 0, :]}[n]
                        ins = pe.transpose(ps[:, 4 + g % 4, P * m:P * m + P], src, ident)
                    ins.then_inc(qt_mm, 1)

            def scores(l, v):
                u = UNITS * l + v
                i, pr = tile_of_unit(v)
                k0, nk = (0, P) if i == 0 else (P, 3 * P)
                if v >= 2:
                    pe.wait_ge(exp_done, u - 1)
                for cc in range(2):
                    ins = pe.matmul(ps[:, 2 * (v % 2) + cc, 0:nk], qT[HD * cc:HD * cc + HD, pr, P * i:P * i + P],
                                    kT[HD * cc:HD * cc + HD, min(pr, 4), k0:k0 + nk], start=True, stop=True)
                ins.then_inc(s_mm, 1)

            def turn_p(l, v):
                u = UNITS * l + v
                i, pr = tile_of_unit(v)
                pe.wait_ge(soft_done, u + 1)
                pe.wait_ge(pT_act, u)
                if gqa_before(u):
                    pe.wait_ge(pT_dve, gqa_before(u))
                for cc in range(1 if pr < 4 else 2):
                    for kb in range(1 if i == 0 else 3):
                        ins = pe.transpose(ps[:, 4 + cc, P * kb:P * kb + P],
                                           prob[:, v % 2, cc, P * kb:P * kb + P], ident)
                ins.then_inc(pT_mm, 1)

            def weigh_v(l, v):
                u = UNITS * l + v
                i, pr = tile_of_unit(v)
                pe.wait_ge(pT_act, u + 1)
                if pr >= 4:
                    pe.wait_ge(pT_dve, gqa_before(u) + 1)
                pe.wait_ge(o_copied, u)
                nb = 1 if i == 0 else 3
                for cc in range(1 if pr < 4 else 2):
                    for kb in range(nb):
                        if pr < 4:
                            c0, w = P * pr, P
                            rhs = (cache_a[:, 1, c0:c0 + w] if kb == 2 else
                                   qkv[:, 0 if i == 0 else kb + 1, AV + c0:AV + c0 + w])
                        else:
                            c0, w = HD * cc, HD
                            rhs = (cache_b[:, 1, c0:c0 + w] if kb == 2 else
                                   qkv[:, 0 if i == 0 else kb + 1, BV + c0:BV + c0 + w])
                        ins = pe.matmul(ps[:, 6, w * cc:w * cc + w], pT[:, v % 2, cc, P * kb:P * kb + P], rhs,
                                        start=(kb == 0), stop=(kb == nb - 1))
                ins.then_inc(o_mm, 1)

            def gate_up(s, half):
                ch, i = divmod(s, NT)
                _, lo, hi = ffn_part(3 * ch + half)
                lo = lo.rearrange("p (k n) -> p k n", k=4)
                hi = hi.rearrange("p (k n) -> p k n", k=4)
                t = slice(P * i, P * i + P)
                for q in range(4):
                    kc = 4 * half + q
                    ins = split_products(ps[:, 6 + s % 2, :], ffn_in_hi[:, kc, t], hT_parts[:, kc, t], hi[:, q, :],
                                         lo[:, q, :], kc == 0, kc == KD - 1)
                if half:
                    ins.then_inc(gu_mm, 1)

            def turn_hidden(s, k):
                pe.wait_ge(hid_ready, s + 1)
                for f in range(2):
                    ins = pe.transpose(ps[:, 6 + k % 2, P * f:P * f + P], hid[:, k % 2, P * f:P * f + P], ident)
                ins.then_inc(hidT_mm, 1)

            def down(s):
                ch, i = divmod(s, NT)
                lo, hi = [w.rearrange("p (f n) -> p f n", f=2) for w in ffn_part(3 * ch + 2)[1:]]
                pe.wait_ge(hidT_rest, s + 1)
                for n in range(2):
                    c = slice(512 * n, 512 * n + 512)
                    for f in range(2):
                        ins = split_products(ps[:, 2 * i + n, :], hidT_hi[:, s % 2, f, :], hidT_lo[:, s % 2, f, :],
                                             hi[:, f, c], lo[:, f, c], ch == 0 and f == 0, ch == NCH - 1 and f == 1)
                return ins

            pe.wait_ge(first_loaded, 80)
            pe.wait_ge(silu_done, 1)
            pe.wait_ge(params_loaded, 128)
            for l in range(DEPTH):
                k0 = first_gu[l]
                if l:
                    pe.wait_ge(params_loaded, 128 * (l + 1))
                for j in range(4):
                    ada_rows(l, j, k0 + j)
                    ada_expand(l, j)
                turn_x(l, 0)
                pe.wait_ge(input_lo, ACT_PARTS * l + 8)
                for n, gs in enumerate(QT_AFTER):
                    project(l, n)
                    turn_qk(l, gs)
                pe.wait_ge(qkv_copied, 15 * l + 15)
                pe.wait_ge(qt_copied, NGROUPS * (l + 1))
                for v in range(UNITS + 2):
                    if v < UNITS:
                        scores(l, v)
                    if 1 <= v <= UNITS:
                        turn_p(l, v - 1)
                    if v >= 2:
                        weigh_v(l, v - 2)
                    q, r = divmod(v, 3)
                    if q < 8 and r == 1:
                        ada_rows(l, 4 + q, k0 + 9 + q)
                    if q < 8 and r == 2:
                        for k in EXPAND_OF[4 + q]:
                            ada_expand(l, k)
                pe.wait_ge(o_copied, UNITS * (l + 1))
                for i in range(NT):
                    for hf in range(2):
                        for m in range(4):
                            ins = pe.transpose(ps[:, 2 * i + hf, P * m:P * m + P],
                                               o[:, i, P * (4 * hf + m):P * (4 * hf + m) + P], ident)
                        ins.then_inc(oT_mm, 1)
                pe.wait_ge(input_lo, ACT_PARTS * l + 14)
                for h in range(10, PROJ_HALVES):
                    project_half(l, h, [2 * i + (h - 10) // 2 for i in range(NT)], lambda i: None, out_mm)
                pe.wait_ge(x_ready, 6 * l + 3)
                for k in range(12, 16):
                    ada_expand(l, k)
                turn_x(l, 1)
                pe.wait_ge(ada_exp_copied, 16 * (l + 1))
                if l == 0:
                    pe.wait_ge(input_lo, ACT_PARTS)
                    for s in range(DENSE + 1):
                        ch, i = divmod(s, NT)
                        if s < DENSE:
                            if i == 0:
                                pe.wait_ge(weight_lo, PROJ_HALVES + 3 * ch + 2)
                            if s >= 2:
                                pe.wait_ge(hidT_rest, s - 1)
                            gate_up(s, 0)
                        if s:
                            turn_hidden(s - 1, s - 1)
                        if s < DENSE:
                            gate_up(s, 1)
                        if s:
                            pc, pi = divmod(s - 1, NT)
                            if pi == 0:
                                pe.wait_ge(weight_lo, PROJ_HALVES + 3 * pc + 3)
                            ins = down(s - 1)
                            if pi == NT - 1:
                                ins.then_inc(chunk_done, 1)

            pe.wait_ge(router_loaded, 16)
            for i in range(NT):
                for kc in range(KD):
                    ins = pe.matmul(ps[:, 0, NE * i:NE * i + NE], hT[:, kc, P * i:P * i + P], w_rt[:, kc, :],
                                    start=(kc == 0), stop=(kc == KD - 1))
            ins.then_inc(logit_mm, 1)
            for i in range(NT):
                for hf in range(2):
                    for m in range(4):
                        ins = pe.transpose(ps[:, 1 + 2 * i + hf, P * m:P * m + P],
                                           hT[:, 4 * hf + m, P * i:P * i + P], ident)
                    ins.then_inc(hTok_mm, 1)
            pe.wait_ge(chosen_ready, 1)
            for i in range(NT):
                for b in range(i):
                    pe.matmul(ps[:, 0, 32 + NE * i:32 + NE * i + NE], cst[:, C_ONES:C_ONES + P], chosen[:, b, :],
                              start=(b == 0), stop=False)
                pe.matmul(ps[:, 0, 32 + NE * i:32 + NE * i + NE], cst[:, C_UP:C_UP + P], chosen[:, i, :],
                          start=(i == 0), stop=True)
            for i in range(NT):
                ins = pe.matmul(ps[:, 0, 64:64 + NE], cst[:, C_ONES:C_ONES + P], chosen[:, i, :],
                                start=(i == 0), stop=(i == NT - 1))
            ins.then_inc(prefix_mm, 1)
            pe.wait_ge(hTok_copied, 6)
            pe.wait_ge(sched_ready, 1)

            def gather(nb, b0):
                def rows(b):
                    if b >= 2:
                        pe.wait_ge(xgT_copied, b0 + (b - 1))
                    for i in range(NT):
                        for n in range(2):
                            ins = pe.matmul(ps[BT * n:BT * n + BT, 6 + b % 2, :], pick[:, i, BT * b:BT * b + BT],
                                            h_tok[:, i, 512 * n:512 * n + 512], start=(i == 0), stop=(i == NT - 1))
                    ins.then_inc(xg_rows_mm, 1)

                def turn(b):
                    pe.wait_ge(xg_rows_copied, b0 + (b + 1))
                    for m in range(4):
                        ins = pe.transpose(ps[:, 6 + b % 2, P * m:P * m + P], xg_rows[:, b % 2, P * m:P * m + P], ident)
                    ins.then_inc(xgT_mm, 1)

                def rest(b):
                    if b + 1 < MAX_BLOCKS:
                        with pe.If(nb > b + 1):
                            rows(b + 1)
                            turn(b)
                            rest(b + 1)
                        with pe.Else():
                            turn(b)
                    else:
                        turn(b)

                rows(0)
                rest(0)

            nb0 = pe.value_load(sched[0:1, 0:1], min_val=1, max_val=MAX_BLOCKS)
            pe.wait_ge(pick_ready, 1)
            gather(nb0, 0)
            with pe.Fori(0, NE) as t:
                nb = pe.value_load(sched[0:1, bass.ds(t, 1)], min_val=1, max_val=MAX_BLOCKS)
                b0 = pe.value_load(sched[0:1, bass.ds(t + (NE + 1), 1)], min_val=0, max_val=MAX_BLOCKS * NE)
                p0 = pe.value_load(sched[0:1, bass.ds(t + (2 * NE + 2), 1)], min_val=0, max_val=MAX_PAIRS * NE)

                def gate_up_half(b, w, half):
                    for kc in range(4 * half, 4 * half + 4):
                        for f in range(2):
                            ins = pe.matmul(ps[BT * f:BT * f + BT, 6 + b % 2, 0:FC].rearrange("p (a f) -> p a f", a=2),
                                            hT[:, kc, BT * b:BT * b + BT], w[:, kc, :, P * f:P * f + P],
                                            start=(kc == 0), stop=(kc == KD - 1))
                    if half:
                        ins.then_inc(gu_mm, 1)

                def turn_half(s, b):
                    pe.wait_ge(hid_ready, s + 1)
                    pe.transpose(ps[:, 6 + b % 2, 0:P], hid[:, b % 2, 0:P], ident).then_inc(hidT_mm, 1)

                def down_half(s, b, wd, first, last):
                    pe.wait_ge(hidT_copied, s + 1)
                    if first and b == 0:
                        pe.wait_ge(spread_added, t * 6 + 1)
                    hT_flat = hidT[:, b % 2, :, :].rearrange("p f t -> p (f t)")
                    for f in range(2):
                        for n in range(2):
                            lo = BT * ((n + b) % 2)
                            ins = pe.matmul(ps[lo:lo + BT, b, :], hT_flat[:, BT * f:BT * f + BT],
                                            wd[:, f, 512 * n:512 * n + 512],
                                            start=(first and f == 0), stop=(last and f == 1))
                    return ins

                pe.wait_ge(xgT_copied, b0 + nb)
                for ch in range(NCH):
                    slot = ch % GU_SLOTS
                    pe.wait_ge(gu_landed[slot], t * (32 * GU_USES[slot]) + 32 * (gu_static[slot] + ch // 3 + 1))
                    pe.wait_ge(d_landed[slot], t * (16 * GU_USES[slot]) + 16 * (GU_USES[slot] + ch // 3 + 1))
                    w, wd = chunk_view(slot), down_view(slot)
                    s0 = b0 * NCH + nb * ch + DENSE
                    first, last = ch == 0, ch == NCH - 1

                    def rest(b):
                        if b + 1 < MAX_BLOCKS:
                            with pe.If(nb > b + 1):
                                gate_up_half(b + 1, w, 0)
                                turn_half(s0 + b, b)
                                gate_up_half(b + 1, w, 1)
                                down_half(s0 + b, b, wd, first, last)
                                rest(b + 1)
                            with pe.Else():
                                turn_half(s0 + b, b)
                                down_half(s0 + b, b, wd, first, last).then_inc(chunk_done, 1)
                        else:
                            turn_half(s0 + b, b)
                            down_half(s0 + b, b, wd, first, last).then_inc(chunk_done, 1)

                    gate_up_half(0, w, 0)
                    gate_up_half(0, w, 1)
                    rest(0)
                nb_next = pe.value_load(sched[0:1, bass.ds(t + 1, 1)], min_val=1, max_val=MAX_BLOCKS)
                pe.wait_ge(pick_ready, t + 2)
                gather(nb_next, b0 + nb)
                pe.wait_ge(xgT_copied, b0 + nb + nb_next)

                def turn_gates(b):
                    pe.wait_ge(pick_g_ready, p0 + (b + 1))
                    if b:
                        pe.wait_ge(pgT_copied, p0 + b)
                    for i in range(NT):
                        pe.transpose(ps[:, 6, P * i:P * i + P], pick_g[:, b % 2, i, :], ident)
                        for h in range(2):
                            ins = pe.matmul(ps[BT * h:BT * h + BT, 7, P * i:P * i + P],
                                            pick_g[:, b % 2, i, BT * (1 - h):BT * (1 - h) + BT], ident,
                                            start=True, stop=True)
                    ins.then_inc(pgT_mm, 1)

                def spread(b, last):
                    for k in range(6):
                        i, n = divmod(k, 2)
                        ins = pe.matmul(ps[:, k, :], pick_gT[:, b, n, i, :], y_sb[:, b, n, :],
                                        start=(b == 0), stop=last)
                        if last:
                            ins.then_inc(spread_mm, 1)

                def spread_from(b):
                    if b + 1 < MAX_PAIRS:
                        with pe.If(nb > 2 * b + 2):
                            turn_gates(b + 1)
                            spread(b, False)
                            spread_from(b + 1)
                        with pe.Else():
                            pe.wait_ge(pgT_copied, p0 + (b + 1))
                            spread(b, True)
                    else:
                        pe.wait_ge(pgT_copied, p0 + (b + 1))
                        spread(b, True)

                turn_gates(0)
                pe.wait_ge(y_copied, b0 + nb)
                spread_from(0)


QT_AFTER = [range(0, 0), range(0, 3), range(3, 6), range(6, 8), range(8, 14)]
EXPAND_OF = {4: [4, 5], 5: [6, 7], 6: [8], 7: [9], 8: [10], 9: [11], 10: [], 11: []}

_INS = ["x_prompt", "x_sample", "cache_a_k", "cache_a_v", "cache_b_k", "cache_b_v", "c", "c_ctx", "w_ada",
        "b_ada", "w_in", "w_out", "diff_lambda", "diff_subln", "qk_norm_gain", "ln_gain", "ln_bias",
        "w_ffn_gate", "w_ffn_up", "w_ffn_down", "w_router", "w_moe_gate", "w_moe_up", "w_moe_down"]
_OUTS = [(1, 128, 1024), (1, 256, 1024), (1, 2, 128, 4, 2, 64), (1, 2, 128, 4, 128),
         (1, 2, 128, 2, 64), (1, 2, 128, 2, 64)]


def kernel(**inputs):
    import concourse.bacc as bacc
    from concourse.bass_utils import run_bass_kernel_spmd

    nc = bacc.Bacc("TRN2", target_bir_lowering=False, num_devices=1)
    arrays, args = {}, []
    for name in _INS:
        arrays[f"in_{name}"] = np.ascontiguousarray(inputs[name])
    arrays["in_consts"] = shape_constants()
    for name, a in arrays.items():
        args.append(nc.dram_tensor(name, a.shape, mybir.dt.from_np(a.dtype), kind="ExternalInput").ap())
    for i, shape in enumerate(_OUTS):
        args.append(nc.dram_tensor(f"out_{i}", shape, F32, kind="ExternalOutput").ap())
    build(nc, *args)
    r = run_bass_kernel_spmd(nc, [arrays], core_ids=[0])
    return tuple(r.results[0][f"out_{i}"] for i in range(len(_OUTS)))
```
